# Optimizing a Trainium2 kernel written in Bass

```python
import math
import jax, jax.numpy as jnp
from jax import lax
import numpy as np

D_MODEL = 1024
BATCH = 1
SEQ = 512
DEPTH = 2

N_A_LAYERS = DEPTH // 2
N_B_LAYERS = DEPTH - N_A_LAYERS

EXPAND = 2
D_INNER = EXPAND * D_MODEL
SSM_HEAD_DIM = 64
SSM_HEADS = D_INNER // SSM_HEAD_DIM
SSM_GROUPS = 8
D_STATE = 128
CONV_K = 4
CHUNK = 128
CONV_DIM = D_INNER + 2 * SSM_GROUPS * D_STATE
IN_PROJ_DIM = D_INNER + CONV_DIM + SSM_HEADS

WINDOWS = (128, 512, 2048)
DILATIONS = (1, 4, 16)
N_ATTN_GROUPS = len(WINDOWS)
HEAD_DIM = 64
N_Q_HEADS = D_MODEL // HEAD_DIM
N_KV_HEADS = 4
Q_WIDTH = N_ATTN_GROUPS * N_Q_HEADS * HEAD_DIM
KV_WIDTH = N_ATTN_GROUPS * N_KV_HEADS * HEAD_DIM
O_WIDTH = N_Q_HEADS * HEAD_DIM
ATTN_BLOCK = 128
ATTN_SCALE = HEAD_DIM ** -0.5

MLP_HIDDEN = 4 * D_MODEL

NORM_EPS = 1e-6
GATED_NORM_EPS = 1e-5

kernel_name = "yoco_mamba2_dilated_attn_hybrid"

def rms_norm(x, eps=NORM_EPS):
    xf = x.astype(jnp.float32)
    return (xf * lax.rsqrt(jnp.mean(xf * xf, axis=-1, keepdims=True) + eps)).astype(x.dtype)

def ada_params(c, w, b, n):
    return jnp.split(jax.nn.silu(c) @ w + b, n, axis=-1)

def modulate(x, shift, scale):
    return rms_norm(x) * (1 + scale[:, None, :]) + shift[:, None, :]

def sq_relu_mlp(h, w1, w2):
    a = jax.nn.relu(h @ w1)
    return (a * a) @ w2

def causal_depthwise_conv(u, w, b):
    out = lax.conv_general_dilated(
        u, w[:, None, :], window_strides=(1,), padding=[(CONV_K - 1, 0)],
        dimension_numbers=('NWC', 'WIO', 'NWC'), feature_group_count=u.shape[-1])
    return out + b

def ssd_chunked(xh, dt, A, Bm, Cm):
    b, s, h, p = xh.shape
    g, n = Bm.shape[2], Bm.shape[3]
    r = h // g
    nc, l = s // CHUNK, CHUNK
    X = (xh.astype(jnp.float32) * dt[..., None]).reshape(b, nc, l, g, r, p)
    a_cs = jnp.cumsum((dt * A).reshape(b, nc, l, g, r), axis=2)
    Bc = Bm.astype(jnp.float32).reshape(b, nc, l, g, n)
    Cc = Cm.astype(jnp.float32).reshape(b, nc, l, g, n)
    causal = jnp.tril(jnp.ones((l, l), dtype=bool))[None, None, :, :, None, None]
    seg = a_cs[:, :, :, None] - a_cs[:, :, None, :]
    Lmat = jnp.exp(jnp.where(causal, seg, -jnp.inf))
    CB = jnp.einsum('bclgn,bcsgn->bclsg', Cc, Bc)
    y_diag = jnp.einsum('bclsg,bclsgr,bcsgrp->bclgrp', CB, Lmat, X)
    decay_to_end = jnp.exp(a_cs[:, :, -1:] - a_cs)
    chunk_states = jnp.einsum('bclgn,bclgr,bclgrp->bcgrpn', Bc, decay_to_end, X)
    chunk_decay = jnp.exp(a_cs[:, :, -1])

    def step(state, inp):
        st, dec = inp
        return state * dec[..., None, None] + st, state

    init = jnp.zeros((b, g, r, p, n), jnp.float32)
    _, prev_states = lax.scan(step, init, (jnp.moveaxis(chunk_states, 1, 0), jnp.moveaxis(chunk_decay, 1, 0)))
    prev_states = jnp.moveaxis(prev_states, 0, 1)
    y_off = jnp.einsum('bclgn,bcgrpn,bclgr->bclgrp', Cc, prev_states, jnp.exp(a_cs))
    return (y_diag + y_off).reshape(b, s, h, p)

def mamba2_mixer(h, w_in, conv_w, conv_b, dt_bias, A_log, D_skip, norm_w, w_out):
    b, s, _ = h.shape
    zxbcdt = h @ w_in
    z = zxbcdt[..., :D_INNER]
    xBC = zxbcdt[..., D_INNER:D_INNER + CONV_DIM]
    dt = zxbcdt[..., D_INNER + CONV_DIM:]
    xBC = jax.nn.silu(causal_depthwise_conv(xBC, conv_w, conv_b))
    xs = xBC[..., :D_INNER].reshape(b, s, SSM_HEADS, SSM_HEAD_DIM)
    Bm = xBC[..., D_INNER:D_INNER + SSM_GROUPS * D_STATE].reshape(b, s, SSM_GROUPS, D_STATE)
    Cm = xBC[..., D_INNER + SSM_GROUPS * D_STATE:].reshape(b, s, SSM_GROUPS, D_STATE)
    dt = jax.nn.softplus(dt.astype(jnp.float32) + dt_bias.astype(jnp.float32))
    A = -jnp.exp(A_log.astype(jnp.float32))
    y = ssd_chunked(xs, dt, A, Bm, Cm)
    y = y + D_skip.astype(jnp.float32)[:, None] * xs.astype(jnp.float32)
    y = y.reshape(b, s, D_INNER).astype(h.dtype) * jax.nn.silu(z)
    y = rms_norm(y.reshape(b, s, SSM_GROUPS, D_INNER // SSM_GROUPS), GATED_NORM_EPS).reshape(b, s, D_INNER)
    return (y * norm_w) @ w_out

def dilated_window_attention(q, k, v, dilation):
    b, s, hq, dh = q.shape
    hkv = k.shape[2]
    rep = hq // hkv
    L = s // dilation
    steps = (WINDOWS[DILATIONS.index(dilation)]) // dilation
    nb = -(-L // ATTN_BLOCK)
    Lp = nb * ATTN_BLOCK

    def to_residue(t):
        t = t.reshape(b, L, dilation, *t.shape[2:]).swapaxes(1, 2).reshape(b * dilation, L, *t.shape[2:])
        return jnp.pad(t, [(0, 0), (0, Lp - L)] + [(0, 0)] * (t.ndim - 2))

    qb = to_residue(q).reshape(-1, nb, ATTN_BLOCK, hkv, rep, dh)
    kb = to_residue(k).reshape(-1, nb, ATTN_BLOCK, hkv, dh)
    vb = to_residue(v).reshape(-1, nb, ATTN_BLOCK, hkv, dh)

    def with_prev(t):
        prev = jnp.pad(t, [(0, 0), (1, 0), (0, 0), (0, 0), (0, 0)])[:, :-1]
        return jnp.concatenate([prev, t], axis=2)

    k_ext, v_ext = with_prev(kb), with_prev(vb)
    scores = jnp.einsum('znqhrd,znkhd->znhrqk', qb, k_ext).astype(jnp.float32) * ATTN_SCALE
    qi = jnp.arange(ATTN_BLOCK)[:, None]
    kj = jnp.arange(2 * ATTN_BLOCK)[None, :]
    dist = ATTN_BLOCK + qi - kj
    key_pos = jnp.arange(nb)[:, None, None] * ATTN_BLOCK - ATTN_BLOCK + kj[None]
    mask = (dist >= 0)[None] & (dist <= steps)[None] & (key_pos >= 0)
    scores = jnp.where(mask[None, :, None, None], scores, -jnp.inf)
    m = jnp.max(scores, axis=-1, keepdims=True)
    pr = jnp.exp(scores - m)
    den = jnp.sum(pr, axis=-1, keepdims=True)
    lse = (m + jnp.log(den))[..., 0]
    out = jnp.einsum('znhrqk,znkhd->znqhrd', pr / den, v_ext.astype(jnp.float32))
    out = out.reshape(-1, Lp, hq, dh)[:, :L]
    lse = jnp.transpose(lse, (0, 1, 4, 2, 3)).reshape(-1, Lp, hq)[:, :L]

    def from_residue(t):
        return t.reshape(b, dilation, L, *t.shape[2:]).swapaxes(1, 2).reshape(b, s, *t.shape[2:])

    return from_residue(out), from_residue(lse)

def shared_kv(x, c, kv_ada_w, kv_ada_b, kv_w, k_norm):
    b, s, _ = x.shape
    shift, scale = ada_params(c, kv_ada_w, kv_ada_b, 2)
    kv = modulate(x, shift, scale) @ kv_w
    k = kv[..., :KV_WIDTH].reshape(b, s, N_ATTN_GROUPS, N_KV_HEADS, HEAD_DIM)
    v = kv[..., KV_WIDTH:].reshape(b, s, N_ATTN_GROUPS, N_KV_HEADS, HEAD_DIM)
    k = rms_norm(k) * k_norm[:, None, :]
    return k, v

def dilated_mixture_mixer(h, k_sh, v_sh, w_q, q_norm, w_o):
    b, s, _ = h.shape
    q = (h @ w_q).reshape(b, s, N_ATTN_GROUPS, N_Q_HEADS, HEAD_DIM)
    q = rms_norm(q) * q_norm[:, None, :]
    outs, lses = [], []
    for g in range(N_ATTN_GROUPS):
        o_g, l_g = dilated_window_attention(q[:, :, g], k_sh[:, :, g], v_sh[:, :, g], DILATIONS[g])
        outs.append(o_g)
        lses.append(l_g)
    w = jax.nn.softmax(jnp.stack(lses), axis=0)
    o = jnp.einsum('gbsh,gbshd->bshd', w, jnp.stack(outs))
    return o.reshape(b, s, O_WIDTH).astype(h.dtype) @ w_o

def setup_inputs(seed: int = 0) -> dict:
    key = jax.random.key(seed)
    ks = jax.random.split(key, 32)

    def nrm(k, shape, scale):
        return jax.random.normal(k, shape, jnp.float32) * scale

    NA, NB = N_A_LAYERS, N_B_LAYERS
    ada_scale = 0.5 * D_MODEL ** -0.5
    dt0 = jnp.exp(jax.random.uniform(ks[7], (NA, SSM_HEADS), jnp.float32, math.log(1e-3), math.log(1e-1)))
    return {
        'x': nrm(ks[0], (BATCH, SEQ, D_MODEL), 1.0),
        'c': nrm(ks[1], (BATCH, D_MODEL), 1.0),
        'a_ada_w': nrm(ks[2], (NA, D_MODEL, 6 * D_MODEL), ada_scale),
        'a_ada_b': nrm(ks[3], (NA, 6 * D_MODEL), 0.01),
        'a_w_in': nrm(ks[4], (NA, D_MODEL, IN_PROJ_DIM), D_MODEL ** -0.5),
        'a_conv_w': nrm(ks[5], (NA, CONV_K, CONV_DIM), CONV_K ** -0.5),
        'a_conv_b': nrm(ks[6], (NA, CONV_DIM), 0.01),
        'a_dt_bias': dt0 + jnp.log(-jnp.expm1(-dt0)),
        'a_A_log': jnp.log(jax.random.uniform(ks[8], (NA, SSM_HEADS), jnp.float32, 1.0, 16.0)),
        'a_D': 1.0 + nrm(ks[9], (NA, SSM_HEADS), 0.1),
        'a_norm_w': 1.0 + nrm(ks[10], (NA, D_INNER), 0.05),
        'a_w_out': nrm(ks[11], (NA, D_INNER, D_MODEL), D_INNER ** -0.5),
        'a_mlp_w1': nrm(ks[12], (NA, D_MODEL, MLP_HIDDEN), D_MODEL ** -0.5),
        'a_mlp_w2': nrm(ks[13], (NA, MLP_HIDDEN, D_MODEL), MLP_HIDDEN ** -0.5),
        'kv_ada_w': nrm(ks[14], (D_MODEL, 2 * D_MODEL), ada_scale),
        'kv_ada_b': nrm(ks[15], (2 * D_MODEL,), 0.01),
        'kv_w': nrm(ks[16], (D_MODEL, 2 * KV_WIDTH), D_MODEL ** -0.5),
        'k_norm': 1.0 + nrm(ks[17], (N_ATTN_GROUPS, HEAD_DIM), 0.05),
        'b_ada_w': nrm(ks[18], (NB, D_MODEL, 6 * D_MODEL), ada_scale),
        'b_ada_b': nrm(ks[19], (NB, 6 * D_MODEL), 0.01),
        'b_w_q': nrm(ks[20], (NB, D_MODEL, Q_WIDTH), D_MODEL ** -0.5),
        'b_q_norm': 1.0 + nrm(ks[21], (NB, N_ATTN_GROUPS, HEAD_DIM), 0.05),
        'b_w_o': nrm(ks[22], (NB, O_WIDTH, D_MODEL), O_WIDTH ** -0.5),
        'b_mlp_w1': nrm(ks[23], (NB, D_MODEL, MLP_HIDDEN), D_MODEL ** -0.5),
        'b_mlp_w2': nrm(ks[24], (NB, MLP_HIDDEN, D_MODEL), MLP_HIDDEN ** -0.5),
    }

def reference(x, c, a_ada_w, a_ada_b, a_w_in, a_conv_w, a_conv_b, a_dt_bias, a_A_log, a_D,
              a_norm_w, a_w_out, a_mlp_w1, a_mlp_w2, kv_ada_w, kv_ada_b, kv_w, k_norm,
              b_ada_w, b_ada_b, b_w_q, b_q_norm, b_w_o, b_mlp_w1, b_mlp_w2):
    k_sh, v_sh = None, None
    for layer in range(DEPTH):
        if layer < N_A_LAYERS:
            i = layer
            sh_m, sc_m, g_m, sh_f, sc_f, g_f = ada_params(c, a_ada_w[i], a_ada_b[i], 6)
            x = x + g_m[:, None, :] * mamba2_mixer(
                modulate(x, sh_m, sc_m), a_w_in[i], a_conv_w[i], a_conv_b[i], a_dt_bias[i],
                a_A_log[i], a_D[i], a_norm_w[i], a_w_out[i])
            x = x + g_f[:, None, :] * sq_relu_mlp(modulate(x, sh_f, sc_f), a_mlp_w1[i], a_mlp_w2[i])
            if layer == N_A_LAYERS - 1:
                k_sh, v_sh = shared_kv(x, c, kv_ada_w, kv_ada_b, kv_w, k_norm)
        else:
            j = layer - N_A_LAYERS
            sh_m, sc_m, g_m, sh_f, sc_f, g_f = ada_params(c, b_ada_w[j], b_ada_b[j], 6)
            x = x + g_m[:, None, :] * dilated_mixture_mixer(
                modulate(x, sh_m, sc_m), k_sh, v_sh, b_w_q[j], b_q_norm[j], b_w_o[j])
            x = x + g_f[:, None, :] * sq_relu_mlp(modulate(x, sh_f, sc_f), b_mlp_w1[j], b_mlp_w2[j])
    return x


_drawn_inputs = setup_inputs


def setup_inputs(seed=0):
    import zlib

    import numpy as np

    out = dict(_drawn_inputs(seed))
    spreads = {}
    factors = {'a_ada_b': 3.154,
     'a_conv_b': 8.0,
     'a_D': 3.491,
     'a_norm_w': 3.877,
     'kv_ada_b': 8.0,
     'k_norm': 8.0,
     'b_ada_b': 4.148,
     'b_q_norm': 8.0}
    for name, (base, spread) in spreads.items():
        noise = np.random.default_rng([zlib.crc32(name.encode()), seed]).standard_normal(out[name].shape)
        drawn = base * np.exp(spread * noise) if base else spread * noise
        out[name] = __import__('jax').numpy.asarray(drawn.astype(out[name].dtype))
    for name, factor in factors.items():
        out[name] = (out[name] * factor).astype(out[name].dtype)
    return out
```

```python
import concourse.bass as bass
from concourse import mybir
from contextlib import ExitStack

F32 = mybir.dt.float32
F32R = mybir.dt.float32r
ALU = mybir.AluOpType
ACT = mybir.ActivationFunctionType
AX = mybir.AxisListType

P = 128
D = 1024
KT = D // P
S = 512
DI = 2 * D
GROUPS = 8
HEADS = 32
HPG = HEADS // GROUPS
NCH = 4
L = S // NCH
HD = 64
TAPS = 4
HID = 4 * D
NG = 3
QH = 16
KVH = 4
REP = QH // KVH
DIL = (1, 4, 16)
NEG = -1.0e30
EPS = 1e-6
GEPS = 1e-5
SLOTS = 4
CW = 256
UNROLL = 4


class Stage:

    def __init__(self, prev, chunks, lpc=1, kg=1):
        self.chunks, self.lpc, self.kg = chunks, lpc, kg
        self.m0 = prev.m0 + prev.chunks if prev else 0
        self.l0 = prev.l0 + prev.chunks * prev.lpc if prev else 0
        self.o0 = prev.o0 + prev.chunks // prev.kg if prev else 0
        self.a0 = prev.a0 + (prev.chunks if prev.lpc == 2 else 0) if prev else 0


class Chain:

    def __init__(self, eng, sem):
        self.eng, self.sem, self.n, self.i, self.per, self.start = eng, sem, 0, 0, 0, 0

    def mark(self, ins):
        ins.then_inc(self.sem, 1)
        self.n += 1

    def wait(self):
        self.eng.wait_ge(self.sem, self.i * self.per + self.n)

    def wait_back(self, n):
        self.eng.wait_ge(self.sem, self.i * self.per + self.n - n)

    def link(self, ins):
        self.mark(ins)
        self.wait()

    def enter(self, i, per):
        self.i, self.per, self.start = i, per, self.n

    def leave(self, times):
        assert self.n - self.start == self.per, (self.n - self.start, self.per)
        self.n += self.per * (times - 1)
        self.i = self.per = 0


def trunk(nc, ins, out, stop=None):
    ctx = ExitStack()
    with ctx:
        cursor = [nc.sbuf_base + (-nc.sbuf_base) % 64]

        def sb(name, shape, dt=F32, at=None):
            size = 4
            for n in shape[1:]:
                size *= n
            if at is None:
                at = cursor[0]
                cursor[0] += size + (-size) % 64
                assert cursor[0] <= nc.sbuf_usable_end, (name, cursor[0])
            return nc.alloc_sbuf_tensor_at(name, shape, dt, offset=at), at

        def pb(name, shape):
            return ctx.enter_context(nc.psum_tensor(name, shape, F32))

        def sem(name):
            return ctx.enter_context(nc.semaphore(name))

        A0_LOADS = 8
        st = {}
        head = Stage(None, 0)
        head.l0, head.a0 = A0_LOADS, A0_LOADS
        order = [("x", 8, 2, 1), ("bc", 8, 2, 1), ("z", 8, 1, 1), ("out", 8, 1, 2),
                 ("m1a", 8, 2, 1), ("m2a", 8, 2, 2), ("m1b", 8, 2, 1), ("m2b", 8, 2, 2),
                 ("kv", 6, 1, 1), ("q", 12, 1, 1), ("o", 4, 1, 1),
                 ("n1a", 8, 1, 1), ("n2a", 8, 1, 2), ("n1b", 8, 1, 1), ("n2b", 8, 1, 2)]
        prev = head
        owner = {s: ("a", s) for s in range(A0_LOADS)}
        for name, chunks, lpc, kg in order:
            prev = st[name] = Stage(prev, chunks, lpc, kg)
            for j in range(chunks):
                owner[prev.l0 + lpc * j] = ("m", prev.m0 + j)
                if lpc == 2:
                    owner[prev.l0 + 2 * j + 1] = ("a", prev.a0 + j)
        LAST = prev.m0 + prev.chunks

        def cols(w, n=CW):
            return w.rearrange("(k p) (n c) -> p n k c", p=P, c=n)

        w_in = ins["a_w_in"][0]
        wz = cols(w_in[:, 0:DI])
        wx = cols(w_in[:, DI:2 * DI])
        wbc = cols(w_in[:, 2 * DI:3 * DI])

        def tall(w, kg):
            return cols(w[kg * D:(kg + 1) * D, :])

        w_out = [tall(ins["a_w_out"][0], n) for n in range(2)]
        mlp = {}
        for tag, pre in (("m", "a"), ("n", "b")):
            mlp[tag + "1a"] = cols(ins[pre + "_mlp_w1"][0][:, 0:HID // 2])
            mlp[tag + "1b"] = cols(ins[pre + "_mlp_w1"][0][:, HID // 2:HID])
            mlp[tag + "2a"] = [tall(ins[pre + "_mlp_w2"][0], n) for n in range(2)]
            mlp[tag + "2b"] = [tall(ins[pre + "_mlp_w2"][0], n) for n in range(2, 4)]
        wkv = cols(ins["kv_w"])
        wq = cols(ins["b_w_q"][0])
        wo = cols(ins["b_w_o"][0])

        def main_src(name, i, u):
            if name in ("out",):
                return w_out[u % 2][:, 2 * i + u // 2]
            if name[1:2] == "2":
                return mlp[name][u % 2][:, 2 * i + u // 2]
            src = {"x": wx, "bc": wbc, "z": wz, "kv": wkv, "q": wq, "o": wo}.get(name)
            if src is None:
                src = mlp[name]
            return src[:, UNROLL * i + u]

        def ada_rows(w):
            return w.rearrange("(k p) (n c) -> p k n c", p=P, c=2 * D)

        ada_a, ada_b, ada_kv = ada_rows(ins["a_ada_w"][0]), ada_rows(ins["b_ada_w"][0]), ada_rows(ins["kv_ada_w"])
        ADA = {"x": (ada_a, 1, 16), "bc": (ada_a, 2, 32), "m1a": (ada_kv, 0, 96), "m2a": (ada_b, 0, 48),
               "m1b": (ada_b, 1, 64), "m2b": (ada_b, 2, 80)}
        SH_M, SC_M, G_M, SH_F, SC_F, G_F = range(0, 48, 8)
        KV_SH, KV_SC, B0 = 96, 104, 48

        xT, _ = sb("xT", [P, KT, S])
        h_hi, AT_H = sb("h_hi", [P, KT, S], F32R)
        h_lo, _ = sb("h_lo", [P, KT, S], F32R)
        conv, AT_BIG = sb("conv", [P, 4 * GROUPS, S])
        big, _ = sb("big", [P, 4 * GROUPS, S], F32R, at=AT_BIG)
        raw, AT_RAW = sb("raw", [P, SLOTS, KT * CW])
        w_lo, _ = sb("w_lo", [P, SLOTS, KT * CW], F32R, at=AT_RAW)
        w_hi, _ = sb("w_hi", [P, 2, KT * CW], F32R)
        ident, _ = sb("ident", [P, P])
        ones, _ = sb("ones", [P, P])
        tri, _ = sb("tri", [P, P])
        negm, _ = sb("negm", [P, P])
        vecs, _ = sb("vecs", [P, 120, 1])
        ada, _ = sb("ada", [P, 112, 1])
        taps, _ = sb("taps", [P, TAPS, HEADS, 1])
        vec2, _ = sb("vec2", [P, 54, 1])
        csil, _ = sb("csil", [P, KT, 1])
        dcol, _ = sb("dcol", [P, 2 * GROUPS, 1])
        dtab, _ = sb("dtab", [P, 4, NCH, GROUPS, HPG])
        half, _ = sb("half", [2, P])
        d_row, _ = sb("d_row", [2, 2 * GROUPS])
        dt_bias, _ = sb("dt_bias", [HEADS, 1])
        a_exp, _ = sb("a_exp", [P, HEADS])
        dt_w, _ = sb("dt_w", [P, KT, HEADS])
        credit, _ = sb("credit", [1, 64])
        MISC = cursor[0]

        def at(base, *shapes):
            found, p = [], base
            for shape in shapes:
                n = 4
                for x in shape:
                    n *= x
                found.append(p)
                p += n + (-n) % 64
            assert p <= nc.sbuf_usable_end, p
            return found

        o_acc, o_ss, o_sq, o_rt, o_rs, o_mod, o_r, = at(
            MISC, [2 * D], [S], [2, S], [S], [S], [2, S], [2, S])
        acc, _ = sb("acc", [P, 2 * D], at=o_acc)
        ssum, _ = sb("ssum", [P, S], at=o_ss)
        sq, _ = sb("sq", [P, 2, S], at=o_sq)
        root, _ = sb("root", [P, S], at=o_rt)
        rstd, _ = sb("rstd", [P, S], at=o_rs)
        mod, _ = sb("mod", [P, 2, S], at=o_mod)
        relu, _ = sb("relu", [P, 2, S], at=o_r)
        pre, _ = sb("pre", [P, 3, P], at=o_r)
        x_in, _ = sb("x_in", [P, NCH, D], at=AT_BIG)

        o_dh, o_dl, o_dT, o_v, o_e, o_z, o_zz, o_p, o_dA, o_cT = at(
            MISC, [KT, P], [KT, P], [S], [P], [P], [P], [P], [P], [P], [P])
        dtw_hi, _ = sb("dtw_hi", [P, KT, P], F32R, at=o_dh)
        dtw_lo, _ = sb("dtw_lo", [P, KT, P], F32R, at=o_dl)
        dt_T, _ = sb("dt_T", [HEADS, S], at=o_dT)
        sp_v, _ = sb("sp_v", [P, P], at=o_v)
        sp_e, _ = sb("sp_e", [P, P], at=o_e)
        sp_z, _ = sb("sp_z", [P, P], at=o_z)
        sp_zz, _ = sb("sp_zz", [P, P], at=o_zz)
        sp_p, _ = sb("sp_p", [P, P], at=o_p)
        dt_a, _ = sb("dt_a", [P, P], at=o_dA)
        cs_T, _ = sb("cs_T", [P, P], at=o_cT)
        cs_dram = nc.dram_tensor("cs_dram", (NCH, GROUPS, HPG, L), F32, kind="Internal").ap()

        (o_stg, o_ab, o_seg, o_cs, o_xd, o_xe, o_bt, o_mt, o_s, o_st2, o_sz, o_gc, o_gq) = at(
            MISC, [4, S], [2, S], [2, S], [2, S], [2, CW], [2, CW], [2, P], [2, S], [CW], [CW], [2, S],
            [2, 64], [2, S])
        stg, _ = sb("stg", [P, 4, S], at=o_stg)
        ab, _ = sb("ab", [P, 2, HPG, L], at=o_ab)
        seg, _ = sb("seg", [P, 2, HPG, L], at=o_seg)
        c_dec, _ = sb("c_dec", [P, 2, HPG, L], at=o_cs)
        x_dt, _ = sb("x_dt", [P, 2, HPG, HD], at=o_xd)
        x_end, _ = sb("x_end", [P, 2, HPG, HD], at=o_xe)
        b_tok, _ = sb("b_tok", [P, 2, P], at=o_bt)
        m_t, _ = sb("m_t", [P, 2, HPG, L], at=o_mt)
        state, _ = sb("state", [P, HPG, HD], at=o_s)
        s_dec, _ = sb("s_dec", [P, HPG, HD], at=o_st2)
        z_act, _ = sb("z_act", [P, 2, S], at=o_sz)
        gcol, _ = sb("gcol", [P, 2, 4, NCH, HPG, 1], at=o_gc)
        g_sq, _ = sb("g_sq", [P, 2, S], at=o_gq)
        fin, _ = sb("fin", [P, NCH, D], at=AT_BIG)

        PS = [pb(f"PS{n}", [P, S]) for n in range(8)]
        BANK = PS[0:4]
        NB, MB = PS[4], PS[5]

        raw_in = [sem(f"raw_in{n}") for n in range(SLOTS)]
        x_loaded = [sem(f"x_loaded{n}") for n in range(NCH)]
        ab_in = [sem(f"ab_in{n}") for n in range(2)]
        names = """vec_in pool_in consts vec_t vec_ok cs_ok xt_t x_new
            hi_ready lo_ready chunk_used ada_used ada_sum ada_tab
            sq_ready ss_done ms_ready root_ready rstd_ready mod_ready h_hi_ready h_ready
            tap0 conv_sum conv_ready relu_ready hid_hi hid_ready dve_own act_own
            dtw_ready dt_ps dt_T_ready dt_t e_in e_ready dtA_ready aexp_ready cum_ready cs_sb dec_in dec_ready
            dtab_ready cs_tt cs_T_ready cs_stored d_ps
            stg_ready cb_ready xdt_ready seg_ready lm_ready ecs_ready cs_ready mt_ready
            yps_ready st_ready state_ready y_ready z_ready yz_ready gsq_ready gsum_ready gms_ready
            groot_ready grstd_ready gmod_ready y_hi y_out
            masks_ready qk_sq qk_sum qk_root qk_rstd qk_done v_perm v_tt v_tok q_staged half_staged staged sc_ready masked max_ready neg_ready
            probs_ready pt_ps pt0_ready pt1_ready pv_ready o_kept stat_kept stat_t sum_t_ready below_top w_exp w_ready
            w_wide mixed o_hi o_ready out_t out_sb out_sem""".split()
        s_ = {n: sem(n) for n in names}

        X0 = {"init": 0, "out": 8, "m2a": 16, "m2b": 24, "o": 32, "n2a": 40, "n2b": 48}
        NORM_OF = {"init": 0, "out": 1, "m2b": 2, "o": 3}
        HID0 = {"m1a": 0, "m1b": 16, "n1a": 32, "n1b": 48}
        CREDIT = {"hid_ready": 2, "mt_ready": 2, "yps_ready": 2, "y_out": 1, "y_ready": 1, "z_ready": 3,
                  "groot_ready": 2, "cb_ready": 1, "cs_ready": 1, "state_ready": 1, "conv_sum": 3, "relu_ready": 3,
                  "masked": 2, "pt_ps": 2, "pt0_ready": 2, "pt1_ready": 1, "pv_ready": 5, "o_kept": 2, "stat_kept": 1}
        POOL_IN, ROWS_IN = 16 * 4, 16 * 11
        CONV0 = {"x": 0, "bc": 16}
        block = ctx.enter_context(nc.Block())
        END = {"A0": "bc", "A1": "out", "A2": "m2b"}.get(stop)
        ACTIVE = []
        for name, *_ in order:
            ACTIVE.append(name)
            if END == name:
                break
        NEXT = dict(zip(ACTIVE, ACTIVE[1:]))

        def tile_at(t):
            return 4 * (t // 2) + t % 2, 4 * (t // 2) + 2 + t % 2

        def bodies(eng, name, body):
            n = st[name].chunks // UNROLL
            if n > 1:
                with eng.Fori(0, n) as i:
                    body(i, UNROLL)
            elif n == 1:
                body(0, UNROLL)
            rest = st[name].chunks - n * UNROLL
            if rest:
                body(n, rest)

        def wait(eng, name, value):
            value = value + CREDIT.get(name, 0)
            eng.wait_ge(s_[name], value)
            if eng.engine in (nc.scalar.engine, nc.gpsimd.engine) and not isinstance(value, int):
                eng.nop(nofuse=True)

        def scan_pool(pool):
            pool.wait_ge(s_["dtab_ready"], 1)
            pool.wait_ge(s_["cs_T_ready"], 1)
            pool.dma_start(cs_dram.rearrange("c g h l -> (c g h) l"), cs_T[:, :]).then_inc(s_["cs_stored"], 16)
            pool.wait_ge(s_["cs_stored"], 16)

            def spread(c, g):
                pool.dma_start(ab[:, c % 2], cs_dram[c, g].partition_broadcast(P)).then_inc(ab_in[c % 2], 16)

            spread(0, 0)
            spread(1, 0)

            def group(g):
                for c in range(NCH):
                    it = NCH * g + c
                    pool.wait_ge(ab_in[c % 2], 32 * g + 16 * (c // 2 + 1))
                    wait(pool, "mt_ready", it - 1)
                    pool.tensor_tensor(seg[:, c % 2], ab[:, c % 2],
                                       negm[:, :].unsqueeze(1).broadcast_to([P, HPG, L]), ALU.add).then_inc(s_["seg_ready"], 1)
                    if c:
                        n = (NCH - 1) * g + c
                        pool.wait_ge(s_["ecs_ready"], n)
                        wait(pool, "yps_ready", it - 1)
                        pool.wait_ge(s_["stg_ready"], g + 1)
                        pool.tensor_tensor(c_dec[:, c % 2], ab[:, c % 2],
                                           stg[:, 3, c * L:(c + 1) * L].unsqueeze(1).broadcast_to([P, HPG, L]),
                                           ALU.mult).then_inc(s_["cs_ready"], 1)
                        wait(pool, "cs_ready", n)
                    else:
                        pool.wait_ge(s_["seg_ready"], it + 1)
                    if c < 2:
                        spread(c + 2, g)
                    elif not (isinstance(g, int) and g == GROUPS - 1):
                        spread(c - 2, g + 1)

            with pool.Fori(0, GROUPS - 1) as g:
                group(g)
            group(GROUPS - 1)


        def conv_tile(name, i, u, t):
            if name == "x":
                return 2 * UNROLL * i + 2 * u + t, 4 * UNROLL * i + 4 * u + t
            return 2 * GROUPS + 2 * UNROLL * i + 2 * u + t, i + 4 * (2 * u + t) + 2

        def step_sizes_act(act):
            wait(act, "dt_ps", 1)
            wait(act, "pool_in", POOL_IN)
            nc.scalar.activation(dt_T[:, :], PS[6][0:HEADS, :], ACT.Identity, bias=dt_bias[:, 0:1]).then_inc(s_["dt_T_ready"], 1)
            nc.scalar.activation(a_exp[:, :], a_exp[:, :], ACT.Exp).then_inc(s_["aexp_ready"], 1)
            wait(act, "e_in", 1)
            nc.scalar.activation(sp_e[:, :], sp_p[:, :], ACT.Exp, scale=-1.0).then_inc(s_["e_ready"], 1)
            wait(act, "dec_in", 1)
            nc.scalar.activation(sp_e[:, :], sp_z[:, :], ACT.Exp).then_inc(s_["dec_ready"], 1)
            nc.scalar.activation(dtab[:, 3].rearrange("p c g h -> p (c g h)"), sp_zz[:, :], ACT.Exp).then_inc(s_["dec_ready"], 1)

        def step_sizes_vec(v, own):
            flat = dtab[:, :, :, :, :].rearrange("p k c g h -> p k (c g h)")
            v.wait_ge(s_["pool_in"], POOL_IN)
            own.mark(nc.vector.memset(dtw_hi[:, :, :].bitcast(F32), 0.0))
            own.link(nc.vector.memset(dtw_lo[:, :, :].bitcast(F32), 0.0))
            own.link(nc.vector.tensor_copy(dtw_hi[:, :, 0:HEADS], dt_w[:, :, :]))
            nc.vector.tensor_tensor(dtw_lo[:, :, 0:HEADS], dt_w[:, :, :], dtw_hi[:, :, 0:HEADS].bitcast(F32),
                                    ALU.subtract).then_inc(s_["dtw_ready"], 1)
            v.wait_ge(s_["dt_t"], 1)
            own.link(nc.vector.tensor_copy(sp_v[:, :], PS[7][:, 0:P]))
            nc.vector.scalar_tensor_tensor(out=sp_p[:, :], in0=sp_v[:, :], scalar=-1.0, in1=sp_v[:, :],
                                           op0=ALU.mult, op1=ALU.max).then_inc(s_["e_in"], 1)
            v.wait_ge(s_["e_ready"], 1)
            own.link(nc.vector.tensor_scalar(sp_z[:, :], sp_e[:, :], 2.0, None, ALU.add))
            own.link(nc.vector.reciprocal(sp_z[:, :], sp_z[:, :]))
            own.link(nc.vector.tensor_tensor(sp_z[:, :], sp_z[:, :], sp_e[:, :], ALU.mult))
            own.link(nc.vector.tensor_tensor(sp_zz[:, :], sp_z[:, :], sp_z[:, :], ALU.mult))
            own.link(nc.vector.tensor_scalar(sp_p[:, :], sp_zz[:, :], 1.0 / 15, None, ALU.mult))
            for n in (13, 11, 9, 7, 5, 3):
                own.link(nc.vector.scalar_tensor_tensor(out=sp_p[:, :], in0=sp_p[:, :], scalar=1.0 / n, in1=sp_zz[:, :],
                                                        op0=ALU.add, op1=ALU.mult))
            own.link(nc.vector.scalar_tensor_tensor(out=sp_p[:, :], in0=sp_p[:, :], scalar=1.0, in1=sp_z[:, :],
                                                    op0=ALU.add, op1=ALU.mult))
            own.link(nc.vector.tensor_scalar(sp_v[:, :], sp_v[:, :], 0.0, None, ALU.max))
            own.link(nc.vector.scalar_tensor_tensor(out=flat[:, 0], in0=sp_p[:, :], scalar=2.0, in1=sp_v[:, :],
                                                    op0=ALU.mult, op1=ALU.add))
            v.wait_ge(s_["aexp_ready"], 1)
            nc.vector.scalar_tensor_tensor(out=dt_a[:, :].rearrange("p (c h) -> p c h", c=NCH),
                                           in0=flat[:, 0].rearrange("p (c h) -> p c h", c=NCH), scalar=-1.0,
                                           in1=a_exp[:, :].unsqueeze(1).broadcast_to([P, NCH, HEADS]),
                                           op0=ALU.mult, op1=ALU.mult).then_inc(s_["dtA_ready"], 1)
            v.wait_ge(s_["cum_ready"], 1)
            nc.vector.tensor_copy(sp_v[:, :], PS[7][:, P:2 * P]).then_inc(s_["cs_sb"], 1)
            own.link(nc.vector.tensor_scalar(flat[:, 1], PS[7][:, P:2 * P], -1.0, None, ALU.mult))
            own.link(nc.vector.tensor_copy(sp_zz[:, :], PS[7][:, 2 * P:3 * P]))
            nc.vector.tensor_tensor(sp_z[:, :], sp_zz[:, :], flat[:, 1], ALU.add).then_inc(s_["dec_in"], 1)
            v.wait_ge(s_["cs_tt"], 1)
            nc.vector.tensor_copy(cs_T[:, :], PS[6][:, 0:P]).then_inc(s_["cs_T_ready"], 1)
            v.wait_ge(s_["d_ps"], 1)
            own.link(nc.vector.tensor_copy(dcol[:, :, 0], MB[:, 0:2 * GROUPS]))
            v.wait_ge(s_["dec_ready"], 2)
            nc.vector.tensor_tensor(flat[:, 2], flat[:, 0], sp_e[:, :], ALU.mult).then_inc(s_["dtab_ready"], 1)

        def step_sizes_pe(pe):
            pe.wait_ge(s_["dtw_ready"], 1)
            pe.wait_ge(s_["pool_in"], POOL_IN)
            for k in range(KT):
                for w, x in ((dtw_hi, h_hi), (dtw_hi, h_lo), (dtw_lo, h_hi)):
                    last = nc.tensor.matmul(PS[6][:, :], w[:, k], x[:, k], start=(k == 0 and w is dtw_hi and x is h_hi),
                                            stop=(k == KT - 1 and w is dtw_lo))
            last.then_inc(s_["dt_ps"], 1)
            pe.wait_ge(s_["dt_T_ready"], 1)
            for c in range(NCH):
                last = nc.tensor.transpose(PS[7][:, c * HEADS:(c + 1) * HEADS], dt_T[:, c * L:(c + 1) * L], ident[0:HEADS, 0:HEADS])
            last.then_inc(s_["dt_t"], 1)
            pe.wait_ge(s_["dtA_ready"], 1)
            nc.tensor.matmul(PS[7][:, P:2 * P], tri[:, :], dt_a[:, :], start=True, stop=True)
            nc.tensor.matmul(PS[7][:, 2 * P:3 * P], ones[:, :], dt_a[:, :], start=True, stop=True).then_inc(s_["cum_ready"], 1)
            pe.wait_ge(s_["cs_sb"], 1)
            nc.tensor.transpose(PS[6][:, 0:P], sp_v[:, :], ident[:, :]).then_inc(s_["cs_tt"], 1)
            nc.tensor.matmul(MB[:, 0:2 * GROUPS], half[:, :], d_row[:, :], start=True, stop=True).then_inc(s_["d_ps"], 1)

        def lag_act(act, g, gp, c):
            if c == 0:
                for t in range(2):
                    wait(act, "yz_ready", 2 * g + t + 1)
                    nc.scalar.activation(g_sq[:, t], conv[:, 4 * g + t], ACT.Square).then_inc(s_["gsq_ready"], 1)
            if c == 1:
                wait(act, "gms_ready", g + 1)
                nc.scalar.activation(g_sq[:, 1], BANK[2 * gp][:, :], ACT.Sqrt, bias=GEPS, scale=1.0 / CW).then_inc(s_["groot_ready"], 1)
            if c == 2:
                for t in range(2):
                    wait(act, "gmod_ready", 2 * g + t + 1)
                    nc.scalar.activation(big[:, 4 * g + 2 + t], z_act[:, t], ACT.Copy).then_inc(s_["y_hi"], 1)

        def scan_act(act, split_next):
            def body(i, units):
                for u in range(units):
                    g = UNROLL * i + u
                    gp = u % 2
                    wait(act, "stg_ready", g + 1)
                    for c in range(NCH):
                        it = NCH * g + c
                        wait(act, "seg_ready", it + 1)
                        for hh in range(HPG):
                            last = nc.scalar.activation(seg[:, c % 2, hh], seg[:, c % 2, hh], ACT.Exp,
                                                        bias=gcol[:, gp, 1, c, hh])
                        last.then_inc(s_["lm_ready"], 1)
                        if c:
                            nc.scalar.activation(ab[:, c % 2], ab[:, c % 2], ACT.Exp).then_inc(s_["ecs_ready"], 1)
                        if c == 0:
                            split_next("z", i, u)
                        if u:
                            lag_act(act, g - 1, 1 - gp, c)
                    wait(act, "chunk_used", st["z"].m0 + g + 1)
                    wait(act, "y_out", 2 * g)
                    for t in range(2):
                        nc.scalar.activation(z_act[:, t], BANK[2 * gp + t][:, :], ACT.Silu).then_inc(s_["z_ready"], 1)
                for c in range(NCH):
                    lag_act(act, UNROLL * i + UNROLL - 1, 1, c)

            bodies(act, "z", body)

        def lag_vec(v, g, gp, c):
            if c == 0:
                wait(v, "y_ready", NCH * g + NCH)
                for t in range(2):
                    wait(v, "z_ready", 2 * g + t + 1)
                    nc.vector.tensor_tensor(conv[:, 4 * g + t], conv[:, 4 * g + t], z_act[:, t], ALU.mult).then_inc(s_["yz_ready"], 1)
            if c == 1:
                v.wait_ge(s_["gsq_ready"], 2 * g + 2)
                nc.vector.tensor_tensor(g_sq[:, 0], g_sq[:, 0], g_sq[:, 1], ALU.add).then_inc(s_["gsum_ready"], 1)
            if c == 2:
                wait(v, "groot_ready", g + 1)
                nc.vector.reciprocal(g_sq[:, 0], g_sq[:, 1]).then_inc(s_["grstd_ready"], 1)
                v.wait_ge(s_["grstd_ready"], g + 1)
                for t in range(2):
                    nc.vector.scalar_tensor_tensor(out=z_act[:, t], in0=conv[:, 4 * g + t], scalar=vec2[:, 32 + 2 * g + t],
                                                   in1=g_sq[:, 0], op0=ALU.mult, op1=ALU.mult).then_inc(s_["gmod_ready"], 1)
            if c == 3:
                for t in range(2):
                    v.wait_ge(s_["y_hi"], 2 * g + t + 1)
                    nc.vector.tensor_tensor(big[:, 4 * g + t], z_act[:, t], big[:, 4 * g + 2 + t].bitcast(F32),
                                            ALU.subtract).then_inc(s_["y_out"], 1)

        def scan_vec(v, own, split_lo_next):
            v.wait_ge(s_["conv_ready"], 4 * GROUPS)
            v.wait_ge(s_["dtab_ready"], 1)
            conv_g = conv[:, :, :].rearrange("p (g f) s -> p g f s", f=4)

            def body(i, units):
                for u in range(units):
                    g = UNROLL * i + u
                    gp = u % 2
                    wait(v, "cb_ready", NCH * g)
                    wait(v, "cs_ready", (NCH - 1) * g)
                    wait(v, "y_ready", NCH * g)
                    own.mark(nc.vector.tensor_copy(gcol[:, gp, :, :, :, 0], dtab[:, :, :, g]))
                    nc.vector.tensor_copy(stg[:, :, :], conv_g[:, g]).then_inc(s_["stg_ready"], 1)
                    own.wait()
                    v.wait_ge(s_["stg_ready"], g + 1)

                    def col(kind, c, n):
                        return gcol[:, gp, kind, c].broadcast_to([P, HPG, n])

                    for c in range(NCH):
                        it = NCH * g + c
                        tb, cp = PS[4 + c % 2], c % 2
                        x_tok = tb[:, 0:CW].rearrange("p (h d) -> p h d", h=HPG)
                        wait(v, "cb_ready", it + 1)
                        last = nc.vector.tensor_tensor(x_dt[:, cp], x_tok, col(0, c, HD), ALU.mult)
                        if c < NCH - 1:
                            nc.vector.tensor_tensor(x_end[:, cp], x_tok, col(2, c, HD), ALU.mult)
                            last = nc.vector.tensor_copy(b_tok[:, cp], tb[:, CW:CW + P])
                        last.then_inc(s_["xdt_ready"], 1)
                        v.wait_ge(s_["lm_ready"], it + 1)
                        nc.vector.tensor_tensor(m_t[:, cp], tb[:, 3 * P:4 * P].unsqueeze(1).broadcast_to([P, HPG, L]),
                                                seg[:, cp], ALU.mult).then_inc(s_["mt_ready"], 1)
                        if c == 0:
                            split_lo_next("z", i, u)
                        if u:
                            lag_vec(v, g - 1, 1 - gp, c)
                        wait(v, "yps_ready", it + 1)
                        for j in range(2):
                            last = nc.vector.scalar_tensor_tensor(
                                out=conv[:, 4 * g + j, c * L:(c + 1) * L], in0=stg[:, j, c * L:(c + 1) * L],
                                scalar=dcol[:, 2 * g + j], in1=PS[6][:, j * L:(j + 1) * L], op0=ALU.mult, op1=ALU.add)
                        last.then_inc(s_["y_ready"], 1)
                        if c < NCH - 1:
                            new = PS[7][:, 0:CW].rearrange("p (h d) -> p h d", h=HPG)
                            if c:
                                own.link(nc.vector.tensor_tensor(s_dec[:, :, :], state[:, :, :], col(3, c, HD), ALU.mult))
                                v.wait_ge(s_["st_ready"], (NCH - 1) * g + c + 1)
                                last = nc.vector.tensor_tensor(state[:, :, :], s_dec[:, :, :], new, ALU.add)
                            else:
                                v.wait_ge(s_["st_ready"], (NCH - 1) * g + c + 1)
                                last = nc.vector.tensor_copy(state[:, :, :], new)
                            last.then_inc(s_["state_ready"], 1)
                            wait(v, "state_ready", (NCH - 1) * g + c + 1)
                for c in range(NCH):
                    lag_vec(v, UNROLL * i + UNROLL - 1, 1, c)

            n = st["z"].chunks // UNROLL
            with v.Fori(0, n) as i:
                own.enter(i, 3 * UNROLL)
                body(i, UNROLL)
            own.leave(n)

        def scan_pe(pe, products):
            wait(pe, "conv_sum", 4 * GROUPS)

            def group_sum(g, gp):
                pe.wait_ge(s_["gsum_ready"], g + 1)
                wait(pe, "z_ready", 2 * g + 2)
                nc.tensor.matmul(BANK[2 * gp][:, :], ones[:, :], g_sq[:, 0], start=True, stop=True).then_inc(s_["gms_ready"], 1)

            def body(i, units):
                for u in range(units):
                    g = UNROLL * i + u
                    gp = u % 2
                    pe.wait_ge(s_["stg_ready"], g + 1)
                    for c in range(NCH):
                        it = NCH * g + c
                        tb, cp = PS[4 + c % 2], c % 2
                        sl = slice(c * L, (c + 1) * L)
                        wait(pe, "mt_ready", it - 1)
                        for j in range(3 if c < NCH - 1 else 2):
                            nc.tensor.transpose(tb[:, j * P:(j + 1) * P], stg[:, j, sl], ident[:, :])
                        nc.tensor.matmul(tb[:, 3 * P:4 * P], stg[:, 2, sl], stg[:, 3, sl], start=True, stop=True).then_inc(s_["cb_ready"], 1)
                        if c == 0:
                            wait(pe, "z_ready", 2 * g - 2)
                            wait(pe, "groot_ready", g - 1)
                        last = products("z", i, u, range(2 * c, 2 * c + 2))
                        if c == NCH - 1:
                            last.then_inc(s_["chunk_used"], 1)
                        if c == 1 and u:
                            group_sum(g - 1, 1 - gp)
                        pe.wait_ge(s_["xdt_ready"], it + 1)
                        wait(pe, "mt_ready", it + 1)
                        wait(pe, "y_ready", it)
                        if c:
                            wait(pe, "cs_ready", (NCH - 1) * g + c)
                            wait(pe, "state_ready", (NCH - 1) * g + c)
                        for hh in range(HPG):
                            dst = PS[6][HD * (hh % 2):HD * (hh % 2) + HD, (hh // 2) * L:(hh // 2 + 1) * L]
                            last = nc.tensor.matmul(dst, x_dt[:, cp, hh], m_t[:, cp, hh], start=True, stop=(c == 0))
                            if c:
                                last = nc.tensor.matmul(dst, state[:, hh], c_dec[:, cp, hh], start=False, stop=True)
                        last.then_inc(s_["yps_ready"], 1)
                        if c < NCH - 1:
                            wait(pe, "state_ready", (NCH - 1) * g + c)
                            nc.tensor.matmul(PS[7][:, 0:CW], b_tok[:, cp], x_end[:, cp].rearrange("p h d -> p (h d)"),
                                             start=True, stop=True).then_inc(s_["st_ready"], 1)
                group_sum(UNROLL * i + UNROLL - 1, 1)

            bodies(pe, "z", body)

        KV_END, Q_END = st["kv"].m0 + st["kv"].chunks, st["q"].m0 + st["q"].chunks
        K_TILES = NG * KVH // 2
        UNITS = NG * KVH
        BLOCKS = S // P
        BODY = 2 * BLOCKS
        q_all, _ = sb("q_all", [P, NG * QH // 2, S], at=AT_BIG)
        k_all, _ = sb("k_all", [P, K_TILES, S], at=AT_BIG + 4 * S * NG * QH // 2)
        o_sqk, o_vp = at(o_acc, [2, S], [2, S])
        qk_s, _ = sb("qk_s", [P, 2, S], at=o_sqk)
        v_order, _ = sb("v_order", [P, 2, S], at=o_vp)
        (o_vt,) = at(o_r + 4 * 2 * S, [NG, BLOCKS, KVH * HD])
        v_all, _ = sb("v_all", [P, NG, BLOCKS, KVH * HD], at=o_vt)
        o_mk, o_mr, o_bd = at(o_vt + 4 * NG * BLOCKS * KVH * HD, [2, P], [P], [P])
        win_mask, _ = sb("win_mask", [P, 2, P], at=o_mk)
        res_mask, _ = sb("res_mask", [P, P], at=o_mr)
        head_ones, _ = sb("head_ones", [P, P], at=o_bd)
        head_row, _ = sb("head_row", [QH, QH // 2, P], at=o_r)
        o_qs, o_ks, o_vs, o_sm, o_pt = at(AT_H, [2, 2, S], [2, S], [2, BLOCKS, HD], [2, REP, 2 * P], [2, 2, S])
        q_u, _ = sb("q_u", [P, 2, 2, S], at=o_qs)
        k_u, _ = sb("k_u", [P, 2, S], at=o_ks)
        v_u, _ = sb("v_u", [P, 2, BLOCKS, HD], at=o_vs)
        probs, _ = sb("probs", [P, 2, REP, 2 * P], at=o_sm)
        probs_t, _ = sb("probs_t", [P, 2, 2, REP, P], at=o_pt)
        o_b1, o_b2, o_b3, o_b4 = at(o_acc, [2, 2, BLOCKS, REP], [2, BLOCKS, REP], [NG, BLOCKS, KVH, REP], [NG, BLOCKS, KVH, REP])
        stat, _ = sb("stat", [P, 2, 2, BLOCKS, REP], at=o_b1)
        neg_max, _ = sb("neg_max", [P, 2, BLOCKS, REP, 1], at=o_b2)
        max_all, _ = sb("max_all", [P, NG, BLOCKS, KVH, REP], at=o_b3)
        sum_all, _ = sb("sum_all", [P, NG, BLOCKS, KVH, REP], at=o_b4)
        o_c1, o_c2, o_c3 = at(AT_BIG + 4 * S * NG * QH // 2, [NG, S], [NG, S], [S])
        w_t, _ = sb("w_t", [QH, NG, S], at=o_c1)
        sum_t, _ = sb("sum_t", [QH, NG, S], at=o_c2)
        top, _ = sb("top", [QH, S], at=o_c3)
        mix_a, _ = sb("mix_a", [P, 2, S], at=o_sqk)
        mix_b, _ = sb("mix_b", [P, 2, S], at=o_vp)

        def by_residue(ap, g):
            return ap.rearrange("p (i r) -> p r i", r=DIL[g])

        def in_residues(ap, g):
            return ap.rearrange("p (r i) -> p r i", r=DIL[g])

        def attention_masks(pool):
            own = s_["masks_ready"]
            wait(pool, "hid_ready", 2 * st["m1a"].chunks + 2 * st["m1b"].chunks)
            wait(pool, "ada_tab", 7)
            pool.memset(win_mask[:, 1], 0.0).then_inc(own, 1)
            pool.memset(head_ones[:, :], 1.0).then_inc(own, 1)
            pool.memset(head_row[:, :, :], 1.0).then_inc(own, 1)
            pool.tensor_copy(win_mask[:, 0], negm[:, :]).then_inc(own, 1)
            pool.wait_ge(own, 4)
            pool.affine_select(out=win_mask[:, 1], in_=win_mask[:, 1], compare_op=ALU.is_ge, fill=NEG, base=0,
                               pattern=[[-1, P]], channel_multiplier=1).then_inc(own, 1)
            pool.affine_select(out=head_ones[:, :], in_=head_ones[:, :], compare_op=ALU.is_ge, fill=0.0, base=0,
                               pattern=[[-HD, 2], [0, HD]], channel_multiplier=1).then_inc(own, 1)
            pool.affine_select(out=head_row[:, :, :], in_=head_row[:, :, :], compare_op=ALU.is_ge, fill=0.0, base=0,
                               pattern=[[P, QH // 2], [1, P]], channel_multiplier=-HD).then_inc(own, 1)
            pool.wait_ge(own, 7)
            pool.affine_select(out=res_mask[:, :], in_=win_mask[:, 1], compare_op=ALU.is_ge, fill=NEG, base=S // DIL[2] - 1,
                               pattern=[[S // DIL[2], P * DIL[2] // S], [0, S // DIL[2]]], channel_multiplier=-1).then_inc(own, 1)
            pool.affine_select(out=head_ones[:, :], in_=head_ones[:, :], compare_op=ALU.is_ge, fill=0.0, base=HD - 1,
                               pattern=[[HD, 2], [0, HD]], channel_multiplier=-1).then_inc(own, 1)
            pool.affine_select(out=head_row[:, :, :], in_=head_row[:, :, :], compare_op=ALU.is_ge, fill=0.0, base=HD - 1,
                               pattern=[[-P, QH // 2], [-1, P]], channel_multiplier=HD).then_inc(own, 1)

        def attention_pool(pool):
            pool.wait_ge(s_["chunk_used"], Q_END)
            pool.wait_ge(s_["qk_done"], K_TILES + NG * QH // 2)
            pool.wait_ge(s_["v_tok"], K_TILES)
            for g in range(NG):
                with pool.Fori(0, KVH // 2) as i:
                    for u in range(2):
                        wait(pool, "pv_ready", BLOCKS * (KVH * g + 2 * i + u - 1))
                        for j in range(2):
                            pool.tensor_copy(in_residues(q_u[:, u, j], g),
                                             by_residue(q_all[:, KT * g + 4 * i + 2 * u + j], g)).then_inc(s_["q_staged"], 1)
                        wait(pool, "q_staged", 2 * (KVH * g + 2 * i + u) + 2)
                        for side in range(2):
                            pool.tensor_copy(k_u[side * HD:(side + 1) * HD, u],
                                             k_all[u * HD:(u + 1) * HD, 2 * g + i]).then_inc(s_["half_staged"], 1)
                            wait(pool, "half_staged", 2 * (KVH * g + 2 * i + u) + side + 1)
                        pool.tensor_copy(v_u[:, u], v_all[:, g, :, :].rearrange("p b (i h d) -> p b i h d", i=2, h=2)[:, :, i, u]).then_inc(s_["staged"], 1)

        def norm_act(act, done, scale, bias):
            for t in range(2):
                wait(act, "qk_sum", done + t + 1)
                nc.scalar.activation(qk_s[:, t], PS[6 + t][:, :], ACT.Sqrt, bias=bias, scale=scale).then_inc(s_["qk_root"], 1)

        def norm_vec(v, done, pair, cols_, dests):
            for t in range(2):
                v.wait_ge(s_["qk_root"], done + t + 1)
                nc.vector.reciprocal(qk_s[:, t], qk_s[:, t]).then_inc(s_["qk_rstd"], 1)
            for t in range(2):
                v.wait_ge(s_["qk_rstd"], done + t + 1)
                dst, src, rs = dests(t), BANK[2 * pair + t][:, :], qk_s[:, t]
                if len(dst.shape) == 3:
                    src, rs = by_residue(src, cols_[1]), by_residue(rs, cols_[1])
                nc.vector.scalar_tensor_tensor(out=dst, in0=src, scalar=vec2[:, cols_[0]], in1=rs,
                                               op0=ALU.mult, op1=ALU.mult).then_inc(s_["qk_done"], 1)

        def sums_pe(pe, done, first=False):
            for t in range(2):
                pe.wait_ge(s_["qk_sq"], done + t + 1)
                if not first:
                    pe.wait_ge(s_["qk_root"], done + t - 1)
                nc.tensor.matmul(PS[6 + t][:, :], head_ones[:, :], qk_s[:, t], start=True, stop=True).then_inc(s_["qk_sum"], 1)

        def blocks_of(g):
            return [(n, n // BLOCKS, n % BLOCKS, 2 if g == 0 and n % BLOCKS else 1) for n in range(BODY)]

        def attention_act(act, name, split_next, norm, residual_chunk):
            if name == "kv":
                norm(2, 2, st["m1b"].m0 + st["m1b"].chunks, 4, KV_SH)
                wait(act, "ada_tab", 7)
                for j in range(st["kv"].chunks):
                    i, u = divmod(j, UNROLL)
                    split_next("kv", i, u)
                    if 0 < j <= K_TILES // 2:
                        norm_act(act, 2 * (j - 1), 1.0 / HD, EPS)
                    m = st["kv"].m0 + j
                    wait(act, "chunk_used", m + 1)
                    for t in range(2):
                        bank = BANK[2 * (j % 2) + t][:, :]
                        if j < K_TILES // 2:
                            if j:
                                wait(act, "qk_done", 2 * j - 1 + t)
                            nc.scalar.activation(qk_s[:, t], bank, ACT.Square).then_inc(s_["qk_sq"], 1)
                        else:
                            n = 2 * j - K_TILES + t
                            if n >= 2:
                                wait(act, "v_tt", n - 1)
                            g = n // 2
                            nc.scalar.activation(in_residues(v_order[:, t], g), by_residue(bank, g), ACT.Copy).then_inc(s_["v_perm"], 1)
            elif name == "q":
                norm(None, 3, KV_END, 5, B0 + SH_M)
                with act.Fori(0, NG) as i:
                    for u in range(UNROLL):
                        c = UNROLL * i + u
                        split_next("q", i, u)
                        if u:
                            norm_act(act, K_TILES + 2 * (c - 1), 1.0, HD * EPS)
                        wait(act, "chunk_used", st["q"].m0 + c + 1)
                        for t in range(2):
                            wait(act, "qk_done", K_TILES + 2 * c - 1 + t)
                            nc.scalar.activation(qk_s[:, t], BANK[2 * (u % 2) + t][:, :], ACT.Square).then_inc(s_["qk_sq"], 1)
                    norm_act(act, K_TILES + 2 * (UNROLL * i + UNROLL - 1), 1.0, HD * EPS)
            else:
                wait(act, "qk_done", K_TILES + NG * QH // 2)
                for g in range(NG):
                    with act.Fori(0, 2) as i:
                        base = BODY * (2 * g + i)
                        blocks = blocks_of(g)
                        wait(act, "stat_kept", 2 * g + i)
                        for step in range(BODY + 1):
                            if step < BODY:
                                n, u, b, nk = blocks[step]
                                wait(act, "neg_ready", base + n + 1)
                                for r in range(REP):
                                    last = nc.scalar.activation(probs[:, n % 2, r, 0:nk * P], probs[:, n % 2, r, 0:nk * P], ACT.Exp,
                                                                bias=neg_max[:, u, b, r], accum_out=stat[:, 1, u, b, r:r + 1])
                                last.then_inc(s_["probs_ready"], 1)
                            if step:
                                n, u, b, nk = blocks[step - 1]
                                wait(act, "pt_ps", base + n + 1)
                                wait(act, "pv_ready", base + n - 1)
                                nc.scalar.activation(probs_t[:, n % 2, 0].rearrange("p r q -> p (r q)"), PS[4 + n % 2][:, :],
                                                     ACT.Copy).then_inc(s_["pt0_ready"], 1)
                for g in range(NG):
                    act.wait_ge(s_["stat_t"], 2 * g + 2)
                    nc.scalar.activation(by_residue(sum_t[:, g], g), in_residues(PS[2 * g + 1][0:QH, :], g), ACT.Copy).then_inc(s_["sum_t_ready"], 1)
                act.wait_ge(s_["below_top"], 1)
                nc.scalar.activation(w_t[:, :, :], w_t[:, :, :], ACT.Exp).then_inc(s_["w_exp"], 1)
                for k in range(KT):
                    act.wait_ge(s_["mixed"], k + 1)
                    nc.scalar.activation(h_hi[:, k], mix_a[:, k % 2], ACT.Copy).then_inc(s_["o_hi"], 1)
                for u in range(st["o"].chunks):
                    split_next("o", 0, u)
                    residual_chunk("o", 0, u)

        def attention_vec(v, own, name, split_next, norm, residual_chunk):
            if name == "kv":
                norm(2, 2, 4, KV_SC)
                for j in range(st["kv"].chunks + 1):
                    i, u = divmod(j, UNROLL)
                    if j < st["kv"].chunks:
                        split_next("kv", i, u)
                    if 0 < j <= K_TILES // 2:
                        g = j - 1
                        norm_vec(v, 2 * g, g % 2, (48 + g, g), lambda t: in_residues(k_all[:, 2 * g + t], g))
                    elif j > K_TILES // 2:
                        g = j - 1 - K_TILES // 2
                        for t in range(2):
                            v.wait_ge(s_["v_tt"], 2 * g + t + 1)
                            nc.vector.tensor_copy(v_all[:, g, :, t * P:(t + 1) * P],
                                                  PS[4 + t][:, :].rearrange("p (b f) -> p b f", b=BLOCKS)).then_inc(s_["v_tok"], 1)
            elif name == "q":
                norm(None, 3, 5, B0 + SC_M)
                with v.Fori(0, NG) as i:
                    for u in range(UNROLL + 1):
                        if u < UNROLL:
                            split_next("q", i, u)
                        if u:
                            c = UNROLL * i + u - 1
                            norm_vec(v, K_TILES + 2 * c, (u - 1) % 2, (51 + i, 0), lambda t: q_all[:, 2 * UNROLL * i + 2 * (u - 1) + t])
            else:
                v.wait_ge(s_["chunk_used"], Q_END)
                for g in range(NG):
                    with v.Fori(0, 2) as i:
                        base = BODY * (2 * g + i)
                        blocks = blocks_of(g)
                        for step in range(BODY + 2):
                            if step < BODY:
                                n, u, b, nk = blocks[step]
                                if n == 0:
                                    wait(v, "stat_kept", 2 * g + i)
                                v.wait_ge(s_["sc_ready"], base + n + 1)
                                wait(v, "pt_ps", base + n - 1)
                                mask = res_mask[:, :] if g == 2 else win_mask[:, :, :].rearrange("p b k -> p (b k)")[:, (2 - nk) * P:]
                                for side in range(2):
                                    last = nc.vector.tensor_tensor(
                                        probs[:, n % 2, side:REP:2, 0:nk * P],
                                        BANK[2 * (n % 2) + side][:, 0:2 * nk * P].rearrange("p (r k) -> p r k", r=2),
                                        mask.unsqueeze(1).broadcast_to([P, 2, nk * P]), ALU.add)
                                last.then_inc(s_["masked"], 1)
                                wait(v, "masked", base + n + 1)
                                nc.vector.tensor_reduce(out=stat[:, 0, u, b, :], in_=probs[:, n % 2, :, 0:nk * P],
                                                        axis=AX.X, op=ALU.max).then_inc(s_["max_ready"], 1)
                                v.wait_ge(s_["max_ready"], base + n + 1)
                                nc.vector.tensor_scalar(neg_max[:, u, b, :, 0], stat[:, 0, u, b, :], -1.0, None, ALU.mult).then_inc(s_["neg_ready"], 1)
                            if 0 < step <= BODY and blocks[step - 1][3] == 2:
                                n, u, b, nk = blocks[step - 1]
                                v.wait_ge(s_["pt_ps"], base + n + 1 + CREDIT["pt_ps"])
                                wait(v, "pv_ready", base + n - 1)
                                nc.vector.tensor_copy(probs_t[:, n % 2, 1].rearrange("p r q -> p (r q)"),
                                                      PS[5 - n % 2][:, :]).then_inc(s_["pt1_ready"], 1)
                            if step >= 2:
                                n, u, b, nk = blocks[step - 2]
                                wait(v, "pv_ready", base + n + 1)
                                for j in range(2):
                                    dst = by_residue(q_all[:, KT * g + 4 * i + 2 * u + j], g)
                                    src = PS[6 + n % 2][:, j * P:(j + 1) * P]
                                    if g == 0:
                                        dst = dst[:, 0, b * P:(b + 1) * P]
                                    elif g == 1:
                                        dst = dst[:, b]
                                    else:
                                        dst = dst[:, 4 * b:4 * b + 4]
                                        src = src.rearrange("p (r i) -> p r i", r=4)
                                    last = nc.vector.tensor_copy(dst, src)
                                last.then_inc(s_["o_kept"], 1)
                        v.wait_ge(s_["probs_ready"], base + BODY)
                        nc.vector.tensor_copy(max_all[:, g, :, :].rearrange("p b (i u) r -> p i u b r", u=2)[:, i], stat[:, 0])
                        nc.vector.tensor_copy(sum_all[:, g, :, :].rearrange("p b (i u) r -> p i u b r", u=2)[:, i], stat[:, 1]).then_inc(s_["stat_kept"], 1)
                for g in range(NG):
                    v.wait_ge(s_["stat_t"], 2 * g + 1)
                    own.mark(nc.vector.tensor_copy(by_residue(w_t[:, g], g), in_residues(PS[2 * g][0:QH, :], g)))
                own.wait()
                own.link(nc.vector.tensor_tensor(top[:, :], w_t[:, 0], w_t[:, 1], ALU.max))
                own.link(nc.vector.tensor_tensor(top[:, :], top[:, :], w_t[:, 2], ALU.max))
                nc.vector.tensor_tensor(w_t[:, :, :], w_t[:, :, :], top[:, :].unsqueeze(1).broadcast_to([QH, NG, S]),
                                        ALU.subtract).then_inc(s_["below_top"], 1)
                v.wait_ge(s_["w_exp"], 1)
                v.wait_ge(s_["sum_t_ready"], NG)
                own.link(nc.vector.tensor_tensor(sum_t[:, :, :], sum_t[:, :, :], w_t[:, :, :], ALU.mult))
                own.link(nc.vector.tensor_tensor(top[:, :], sum_t[:, 0], sum_t[:, 1], ALU.add))
                own.link(nc.vector.tensor_tensor(top[:, :], top[:, :], sum_t[:, 2], ALU.add))
                own.link(nc.vector.reciprocal(top[:, :], top[:, :]))
                nc.vector.tensor_tensor(w_t[:, :, :], w_t[:, :, :], top[:, :].unsqueeze(1).broadcast_to([QH, NG, S]),
                                        ALU.mult).then_inc(s_["w_ready"], 1)
                for k in range(KT + 1):
                    if k < KT:
                        if k >= 2:
                            v.wait_ge(s_["o_hi"], k - 1)
                            v.wait_ge(s_["o_ready"], k - 1)
                        a, b = mix_a[:, k % 2], mix_b[:, k % 2]
                        for g in range(NG):
                            v.wait_ge(s_["w_wide"], NG * (k + 1))
                            own.mark(nc.vector.tensor_tensor(a if g == 0 else b, q_all[:, KT * g + k], PS[NG * (k % 2) + g][:, :], ALU.mult))
                            if g:
                                own.wait()
                                ins_ = nc.vector.tensor_tensor(a, a, b, ALU.add)
                                if g < NG - 1:
                                    own.link(ins_)
                                else:
                                    ins_.then_inc(s_["mixed"], 1)
                    if k:
                        v.wait_ge(s_["o_hi"], k)
                        v.wait_ge(s_["mixed"], k)
                        nc.vector.tensor_tensor(h_lo[:, k - 1], mix_a[:, (k - 1) % 2], h_hi[:, k - 1].bitcast(F32), ALU.subtract).then_inc(s_["o_ready"], 1)
                for u in range(st["o"].chunks):
                    split_next("o", 0, u)
                    residual_chunk("o", 0, u)

        def attention_pe(pe, name, products, norm, before):
            if name == "kv":
                norm(2)
                wait(pe, *before)
                pe.wait_ge(s_["masks_ready"], 10)
                for j in range(st["kv"].chunks + 1):
                    i, u = divmod(j, UNROLL)
                    chunk = j < st["kv"].chunks
                    v_j = j - 1 - K_TILES // 2
                    if chunk and j >= 2:
                        if j - 2 < K_TILES // 2:
                            pe.wait_ge(s_["qk_done"], 2 * (j - 1))
                        else:
                            pe.wait_ge(s_["v_perm"], 2 * (j - 1) - K_TILES)
                    if chunk:
                        products("kv", i, u, range(0, KT // 2),
                                 ready=(lambda k: pe.wait_ge(s_["h_ready"], KT * 2 + k + 1)) if j == 0 else None)
                        if j == 0:
                            last = products("kv", i, u, range(KT // 2, KT), ready=lambda k: pe.wait_ge(s_["h_ready"], KT * 2 + k + 1))
                    if 0 < j <= K_TILES // 2:
                        sums_pe(pe, 2 * (j - 1), first=(j == 1))
                    elif v_j >= 0:
                        for t in range(2):
                            pe.wait_ge(s_["v_perm"], 2 * v_j + t + 1)
                            if v_j:
                                pe.wait_ge(s_["v_tok"], 2 * v_j - 1 + t)
                            for b in range(BLOCKS):
                                last_t = nc.tensor.transpose(PS[4 + t][:, b * P:(b + 1) * P], v_order[:, t, b * P:(b + 1) * P], ident[:, :])
                            last_t.then_inc(s_["v_tt"], 1)
                    if chunk:
                        if j:
                            last = products("kv", i, u, range(KT // 2, KT))
                        last.then_inc(s_["chunk_used"], 1)
                return None
            if name == "q":
                pe.wait_ge(s_["v_perm"], K_TILES)
                pe.wait_ge(s_["h_ready"], KT * 4)
                with pe.Fori(0, NG) as i:
                    for u in range(UNROLL):
                        c = UNROLL * i + u
                        pe.wait_ge(s_["qk_done"], K_TILES + 2 * (c - 1))
                        products("q", i, u, range(0, KT // 2))
                        if u:
                            sums_pe(pe, K_TILES + 2 * (c - 1))
                        products("q", i, u, range(KT // 2, KT)).then_inc(s_["chunk_used"], 1)
                    sums_pe(pe, K_TILES + 2 * (UNROLL * i + UNROLL - 1))
                return None
            pe.wait_ge(s_["qk_done"], K_TILES + NG * QH // 2)
            pe.wait_ge(s_["v_tok"], K_TILES)
            for g in range(NG):
                if g == 1:
                    wait(pe, "pt0_ready", 2 * BODY)
                with pe.Fori(0, 2) as i:
                    base = BODY * (2 * g + i)
                    blocks = blocks_of(g)
                    for step in range(BODY + 2):
                        if step < BODY:
                            n, u, b, nk = blocks[step]
                            if b == 0:
                                pe.wait_ge(s_["staged"], KVH * g + 2 * i + u + 1)
                            wait(pe, "masked", base + n - 1)
                            for r in range(REP):
                                half_ = slice((r % 2) * HD, (r % 2) * HD + HD)
                                dst = BANK[2 * (n % 2) + r % 2][:, (r // 2) * nk * P:(r // 2 + 1) * nk * P]
                                last = nc.tensor.matmul(dst, q_u[half_, u, r // 2, b * P:(b + 1) * P],
                                                        k_u[half_, u, (b + 1 - nk) * P:(b + 1) * P], start=True, stop=True)
                            last.then_inc(s_["sc_ready"], 1)
                        if 0 < step <= BODY:
                            n, u, b, nk = blocks[step - 1]
                            pe.wait_ge(s_["probs_ready"], base + n + 1)
                            if g == 0:
                                wait(pe, "pt0_ready", base + n)
                                wait(pe, "pt1_ready", (BLOCKS - 1) * (2 * i + u) + max(b - 1, 0))
                            else:
                                wait(pe, "pt0_ready", base + n - 1)
                            for kb in range(nk):
                                bank = PS[4 + n % 2] if kb == 0 else PS[5 - n % 2]
                                for r in range(REP):
                                    last = nc.tensor.transpose(bank[:, r * P:(r + 1) * P], probs[:, n % 2, r, kb * P:(kb + 1) * P], ident[:, :])
                            last.then_inc(s_["pt_ps"], 1)
                        if step >= 2:
                            n, u, b, nk = blocks[step - 2]
                            wait(pe, "pt0_ready", base + n + 1)
                            if nk == 2:
                                wait(pe, "pt1_ready", (BLOCKS - 1) * (2 * i + u) + b)
                            wait(pe, "o_kept", base + n - 1)
                            for r in range(REP):
                                side, j = r % 2, r // 2
                                for kb in range(nk):
                                    last = nc.tensor.matmul(PS[6 + n % 2][side * HD:(side + 1) * HD, j * P:(j + 1) * P],
                                                            v_u[:, u, b + 1 - nk + kb], probs_t[:, n % 2, kb, r],
                                                            start=(kb == 0), stop=(kb == nk - 1))
                            last.then_inc(s_["pv_ready"], 1)
            wait(pe, "stat_kept", 2 * NG)
            wait(pe, "o_kept", BODY * 2 * NG)
            for g in range(NG):
                for kind, src in enumerate((max_all, sum_all)):
                    for b in range(BLOCKS):
                        last = nc.tensor.transpose(PS[2 * g + kind][0:QH, b * P:(b + 1) * P],
                                                   src[:, g, b].rearrange("p h r -> p (h r)"), ident[:, :])
                    last.then_inc(s_["stat_t"], 1)
            pe.wait_ge(s_["w_ready"], 1)
            for k in range(KT):
                for g in range(NG):
                    if k >= 2:
                        pe.wait_ge(s_["mixed"], k - 1)
                    nc.tensor.matmul(PS[NG * (k % 2) + g][:, :], head_row[:, k], w_t[:, g], start=True, stop=True).then_inc(s_["w_wide"], 1)
            for u in range(st["o"].chunks):
                if u == 0:
                    pe.wait_ge(s_["mixed"], KT)
                else:
                    wait(pe, "x_new", X0["o"] + 2 * (u - 1))
                products("o", 0, u, ready=(lambda k: pe.wait_ge(s_["o_ready"], k + 1)) if u == 0 else None).then_inc(s_["chunk_used"], 1)
            return ("x_new", X0["o"] + KT)

        @block.sync
        def _(sp):
            vec_rows = [(0, 48, 0, ins["a_ada_b"][0]), (48, 96, 0, ins["b_ada_b"][0]), (96, 112, 0, ins["kv_ada_b"]),
                        (112, 120, 0, ins["c"][0]), (0, 32, 2, ins["a_conv_b"][0]), (32, 48, 2, ins["a_norm_w"][0])]
            for a, b, j, src in vec_rows:
                sp.dma_start(pre[a:b, j], src.rearrange("(n p) -> n p", p=P)).then_inc(s_["vec_in"], 16)
            sp.dma_start(pre[:, 1], ins["a_conv_w"][0].rearrange("t (n p) -> (t n) p", p=P)).then_inc(s_["vec_in"], 16)
            for r, src in ((48, ins["k_norm"]), (51, ins["b_q_norm"][0])):
                for side in range(2):
                    sp.dma_start(pre[r:r + NG, 2, side * HD:(side + 1) * HD], src).then_inc(s_["vec_in"], 16)

            def load(s, src, i, per):
                slot = s % SLOTS
                if isinstance(i, int):
                    if s + i * per >= SLOTS:
                        kind, n = owner[s + i * per - SLOTS]
                        sp.wait_ge(s_["chunk_used" if kind == "m" else "ada_used"], n + 1)
                else:
                    kind, n = owner[s - SLOTS]
                    sp.wait_ge(s_["chunk_used" if kind == "m" else "ada_used"], n + 1 + i * UNROLL)
                dst = raw[:, slot].rearrange("p (k c) -> p k c", c=CW) if len(src.shape) == 3 else raw[:, slot]
                sp.dma_start(dst, src).then_inc(raw_in[slot], 16)

            for k in range(A0_LOADS):
                if k == 2:
                    for b in range(NCH):
                        sp.dma_start(x_in[:, b], ins["x"][0, b * P:(b + 1) * P, :]).then_inc(x_loaded[b], 16)
                load(k, ada_a[:, k, 0], 0, 0)

            def regular(name):
                s = st[name]
                per = UNROLL * s.lpc
                return s.chunks % UNROLL == 0 and all(
                    owner[s.l0 + u - SLOTS + i * per] == (owner[s.l0 + u - SLOTS][0], owner[s.l0 + u - SLOTS][1] + i * UNROLL)
                    for u in range(per) for i in range(s.chunks // UNROLL))

            for name in ACTIVE:
                s = st[name]

                def body(i, units):
                    for u in range(units):
                        load(s.l0 + s.lpc * u, main_src(name, i, u), i, UNROLL * s.lpc)
                        if s.lpc == 2:
                            w, g, _ = ADA[name]
                            load(s.l0 + 2 * u + 1, w[:, UNROLL * i + u, g], i, UNROLL * s.lpc)

                if regular(name):
                    bodies(sp, name, body)
                else:
                    for i in range(0, s.chunks, UNROLL):
                        body(i // UNROLL, min(UNROLL, s.chunks - i))
            for b in range(NCH):
                sp.wait_ge(s_["out_sb"], 2 * (b + 1))
                sp.dma_start(out[0, b * P:(b + 1) * P, :], fin[:, b]).then_inc(s_["out_sem"], 16)
            sp.wait_ge(s_["out_sem"], 16 * NCH)

        @block.gpsimd
        def _(pool):
            pool.dma_start(dt_bias[:, :], ins["a_dt_bias"].rearrange("a h -> h a"), allow_slow_non_contiguous=True).then_inc(s_["pool_in"], 16)
            pool.dma_start(a_exp[:, :], ins["a_A_log"][0].partition_broadcast(P)).then_inc(s_["pool_in"], 16)
            pool.dma_start(d_row[:, :], ins["a_D"][0].rearrange("(t two) -> two t", two=2), allow_slow_non_contiguous=True).then_inc(s_["pool_in"], 16)
            pool.dma_start(dt_w[:, :, :], w_in[:, 3 * DI:3 * DI + HEADS].rearrange("(k p) c -> p k c", p=P)).then_inc(s_["pool_in"], 16)
            own = s_["consts"]
            pool.memset(ident[:, :], 0.0).then_inc(own, 1)
            pool.memset(ones[:, :], 1.0).then_inc(own, 1)
            pool.memset(tri[:, :], 1.0).then_inc(own, 1)
            pool.memset(negm[:, :], 0.0).then_inc(own, 1)
            pool.memset(half[:, :], 1.0).then_inc(own, 1)
            pool.memset(ssum[:, :], 0.0).then_inc(own, 1)
            pool.wait_ge(own, 6)
            pool.affine_select(out=ident[:, :], in_=ident[:, :], compare_op=ALU.not_equal, fill=1.0, base=0,
                               pattern=[[-1, P]], channel_multiplier=1).then_inc(own, 1)
            pool.affine_select(out=tri[:, :], in_=tri[:, :], compare_op=ALU.is_ge, fill=0.0, base=0,
                               pattern=[[1, P]], channel_multiplier=-1).then_inc(own, 1)
            pool.affine_select(out=negm[:, :], in_=negm[:, :], compare_op=ALU.is_ge, fill=NEG, base=0,
                               pattern=[[1, P]], channel_multiplier=-1).then_inc(own, 1)
            pool.affine_select(out=half[:, :], in_=half[:, :], compare_op=ALU.is_ge, fill=0.0, base=0,
                               pattern=[[1, P]], channel_multiplier=-HD).then_inc(own, 1)
            pool.wait_ge(own, 10)
            pool.affine_select(out=half[:, :], in_=half[:, :], compare_op=ALU.is_ge, fill=0.0, base=HD - 1,
                               pattern=[[-1, P]], channel_multiplier=HD).then_inc(own, 1)

            def add_square(n, k, slot, first=False):
                if first and n:
                    pool.wait_ge(s_["ms_ready"], n)
                pool.wait_ge(s_["sq_ready"], KT * n + k + 1)
                if first:
                    pool.tensor_copy(ssum[:, :], sq[:, slot]).then_inc(s_["ss_done"], 1)
                else:
                    pool.wait_ge(s_["ss_done"], KT * n + k)
                    pool.tensor_tensor(ssum[:, :], ssum[:, :], sq[:, slot], ALU.add).then_inc(s_["ss_done"], 1)

            def norm_of(n):
                for k in range(KT):
                    add_square(n, k, k % 2, first=(k == 0))

            for at_, name in enumerate(n for n, count in CREDIT.items() for _ in range(count)):
                pool.memset(credit[:, at_:at_ + 1], 0.0).then_inc(s_[name], 1)
            norm_of(0)
            for name in ACTIVE:
                if name == "z":
                    scan_pool(pool)
                if name == "kv":
                    attention_masks(pool)
                if name == "o":
                    attention_pool(pool)
                if name in NORM_OF:
                    norm_of(NORM_OF[name])

        @block.scalar
        def _(act):
            def split_hi(s, i, u):
                slot = (s.l0 + s.lpc * u) % SLOTS
                act.wait_ge(raw_in[slot], 16 * ((s.l0 + s.lpc * u) // SLOTS + i * s.lpc + 1))
                m = s.m0 + u + UNROLL * i
                if s.m0 + u >= 2:
                    wait(act, "chunk_used", m - 1)
                nc.scalar.activation(w_hi[:, (s.m0 + u) % 2], raw[:, slot], ACT.Copy).then_inc(s_["hi_ready"], 1)

            def split_next(name, i, u):
                last = name not in NEXT and u == UNROLL - 1
                s = st[name]
                if not last:
                    split_hi(s, i, u + 1)
                elif isinstance(i, int) and UNROLL * i + u + 1 < s.chunks:
                    split_hi(s, i, u + 1)

            def square(n, k, slot, src):
                if n or k >= 2:
                    wait(act, "ss_done", KT * n + k - 1)
                nc.scalar.activation(sq[:, slot], src, ACT.Square).then_inc(s_["sq_ready"], 1)

            def norm(n, v, free, table, shift):
                if n is not None:
                    wait(act, "ms_ready", n + 1)
                    if n:
                        wait(act, "rstd_ready", n)
                    nc.scalar.activation(root[:, :], NB[:, :], ACT.Sqrt, bias=EPS, scale=1.0 / D).then_inc(s_["root_ready"], 1)
                if free:
                    wait(act, "chunk_used", free)
                wait(act, "ada_tab", table)
                for k in range(KT):
                    wait(act, "mod_ready", KT * v + k + 1)
                    nc.scalar.activation(h_hi[:, k], mod[:, k % 2], ACT.Identity, bias=ada[:, shift + k]).then_inc(s_["h_hi_ready"], 1)

            wait(act, "vec_ok", 3)
            nc.scalar.activation(csil[:, :, 0], vecs[:, 112:120, 0], ACT.Silu).then_inc(s_["cs_ok"], 1)
            for k in range(KT):
                wait(act, "x_new", k + 1)
                square(0, k, k % 2, xT[:, k])
            split_hi(st["x"], 0, 0)
            norm(0, 0, 0, 1, SH_M)

            def conv_chunk(name, i, u):
                s = st[name]
                m = s.m0 + UNROLL * i + u
                done = CONV0[name] + 2 * (UNROLL * i + u)
                wait(act, "chunk_used", m + 1)
                for t in range(2):
                    tile, dst = conv_tile(name, i, u, t)
                    nc.scalar.activation(conv[:, dst], BANK[2 * (u % 2) + t][:, :], ACT.Identity,
                                         bias=vec2[:, tile], scale=taps[:, TAPS - 1, tile]).then_inc(s_["tap0"], 1)
                for t in range(2):
                    _, dst = conv_tile(name, i, u, t)
                    wait(act, "conv_sum", done + t + 1)
                    nc.scalar.activation(conv[:, dst], conv[:, dst], ACT.Silu).then_inc(s_["conv_ready"], 1)

            def hidden_chunk(name, i, u):
                s = st[name]
                done = HID0[name] + 2 * (UNROLL * i + u)
                wait(act, "chunk_used", s.m0 + UNROLL * i + u + 1)
                for t in range(2):
                    wait(act, "hid_ready", done + t - 1)
                    nc.scalar.activation(relu[:, t], BANK[2 * (u % 2) + t][:, :], ACT.Relu).then_inc(s_["relu_ready"], 1)
                for t in range(2):
                    hi = 4 * UNROLL * i + 4 * u + 2 + t
                    wait(act, "relu_ready", done + t + 1)
                    nc.scalar.activation(big[:, hi], relu[:, t], ACT.Square).then_inc(s_["hid_hi"], 1)

            def residual_chunk(name, i, u):
                if name in NORM_OF and (u % st[name].kg == st[name].kg - 1):
                    per = UNROLL // st[name].kg
                    for t in range(2):
                        k = 2 * (per * i + u // st[name].kg) + t
                        wait(act, "x_new", X0[name] + k + 1)
                        square(NORM_OF[name], k, t, xT[:, k])

            for name in ACTIVE:
                if name == "z":
                    step_sizes_act(act)
                    scan_act(act, split_next)
                    continue
                if name in ("kv", "q", "o"):
                    attention_act(act, name, split_next, norm, residual_chunk)
                    continue
                if name in ("m1a", "n1a"):
                    b = name == "n1a"
                    norm(3 if b else 1, 4 if b else 1, st["o" if b else "z"].m0 + st["o" if b else "z"].chunks, 7 if b else 3,
                         (B0 if b else 0) + SH_F)

                def body(i, units):
                    for u in range(units):
                        split_next(name, i, u)
                        if name in ("x", "bc"):
                            conv_chunk(name, i, u)
                        elif name in HID0:
                            hidden_chunk(name, i, u)
                        else:
                            residual_chunk(name, i, u)

                if name not in NEXT:
                    n = st[name].chunks // UNROLL
                    if n > 1:
                        for i in range(n):
                            body(i, UNROLL)
                else:
                    bodies(act, name, body)
        @block.vector
        def _(v):
            own = Chain(v, s_["dve_own"])

            def split_lo(s, i, u):
                slot = (s.l0 + s.lpc * u) % SLOTS
                v.wait_ge(s_["hi_ready"], s.m0 + u + UNROLL * i + 1)
                nc.vector.tensor_tensor(w_lo[:, slot], raw[:, slot], w_hi[:, (s.m0 + u) % 2].bitcast(F32),
                                        ALU.subtract).then_inc(s_["lo_ready"], 1)

            def split_next(name, i, u):
                s = st[name]
                if not (name not in NEXT and u == UNROLL - 1) or (isinstance(i, int) and UNROLL * i + u + 1 < s.chunks):
                    split_lo(s, i, u + 1)

            def ada_step(load, k, a, per, i):
                slot = load % SLOTS
                v.wait_ge(raw_in[slot], 16 * (load // SLOTS + i * per // SLOTS + 1) if isinstance(i, int)
                          else 16 * (load // SLOTS + 1) + i * (16 * per // SLOTS))
                if not isinstance(i, int) or i or a:
                    v.wait_ge(s_["ada_used"], a + i * UNROLL)
                nc.vector.scalar_tensor_tensor(out=acc[:, :], in0=raw[:, slot], scalar=csil[:, k], in1=acc[:, :],
                                               op0=ALU.mult, op1=ALU.add).then_inc(s_["ada_used"], 1)

            def ada_begin(n):
                if n:
                    v.wait_ge(s_["ada_sum"], n)
                own.link(nc.vector.memset(acc[:, :], 0.0))

            def ada_end(n, col):
                v.wait_ge(s_["ada_sum"], n + 1)
                nc.vector.tensor_tensor(ada[:, col:col + 16, 0], MB[:, 0:16], vecs[:, col:col + 16, 0], ALU.add).then_inc(s_["ada_tab"], 1)

            def norm(n, v_, table, scale):
                if n is not None:
                    v.wait_ge(s_["root_ready"], n + 1)
                    nc.vector.reciprocal(rstd[:, :], root[:, :]).then_inc(s_["rstd_ready"], 1)
                    v.wait_ge(s_["rstd_ready"], n + 1)
                v.wait_ge(s_["ada_tab"], table)

                def scaled(k):
                    if k >= 2:
                        v.wait_ge(s_["h_ready"], KT * v_ + k - 1)
                    nc.vector.scalar_tensor_tensor(out=mod[:, k % 2], in0=xT[:, k], scalar=ada[:, scale + k], in1=rstd[:, :],
                                                   op0=ALU.mult, op1=ALU.mult).then_inc(s_["mod_ready"], 1)

                scaled(0)
                for k in range(KT):
                    if k + 1 < KT:
                        scaled(k + 1)
                    v.wait_ge(s_["h_hi_ready"], KT * v_ + k + 1)
                    v.wait_ge(s_["mod_ready"], KT * v_ + k + 1)
                    nc.vector.scalar_tensor_tensor(out=h_lo[:, k], in0=mod[:, k % 2], scalar=ada[:, scale - KT + k],
                                                   in1=h_hi[:, k].bitcast(F32), op0=ALU.add, op1=ALU.subtract).then_inc(s_["h_ready"], 1)

            v.wait_ge(s_["vec_t"], 3)
            vt = vecs[:, :, 0]
            nc.vector.tensor_copy(vt, MB[:, 0:120]).then_inc(s_["vec_ok"], 1)
            nc.vector.tensor_copy(taps[:, :, :, 0], MB[:, P:2 * P].rearrange("p (t n) -> p t n", t=TAPS)).then_inc(s_["vec_ok"], 1)
            nc.vector.tensor_copy(vec2[:, :, 0], MB[:, 2 * P:2 * P + 54]).then_inc(s_["vec_ok"], 1)
            v.wait_ge(s_["vec_ok"], 3)
            for col in (SC_M, SC_F, B0 + SC_M, B0 + SC_F, KV_SC):
                own.link(nc.vector.tensor_scalar(vecs[:, col:col + KT, 0], vecs[:, col:col + KT, 0], 1.0, None, ALU.add))
            ada_begin(0)
            v.wait_ge(s_["cs_ok"], 1)
            for k in range(A0_LOADS):
                if k >= 2:
                    for t in ((2 * (k - 2), 2 * (k - 2) + 1) if k < 6 else ()):
                        v.wait_ge(s_["xt_t"], t + 1)
                        nc.vector.tensor_copy(xT[:, t], BANK[t % 4][:, :]).then_inc(s_["x_new"], 1)
                ada_step(k, k, k, 0, 0)
            split_lo(st["x"], 0, 0)
            ada_end(0, 0)
            norm(0, 0, 1, SC_M)

            def conv_chunk(name, i, u):
                banks = [BANK[2 * (u % 2) + t] for t in range(2)]
                tiles = [conv_tile(name, i, u, t) for t in range(2)]
                done = CONV0[name] + 2 * (UNROLL * i + u)
                for shift in range(1, TAPS):
                    for t in range(2):
                        tile, dst = tiles[t]
                        if shift == 1:
                            v.wait_ge(s_["tap0"], done + t + 1)
                        else:
                            own.wait_back(1 if shift < TAPS - 1 else 1 - t)
                        ins_ = nc.vector.scalar_tensor_tensor(
                            out=conv[:, dst, shift:S], in0=banks[t][:, 0:S - shift], scalar=taps[:, TAPS - 1 - shift, tile],
                            in1=conv[:, dst, shift:S], op0=ALU.mult, op1=ALU.add)
                        if shift < TAPS - 1:
                            own.mark(ins_)
                        else:
                            ins_.then_inc(s_["conv_sum"], 1)

            def hidden_chunk(name, i, u):
                done = HID0[name] + 2 * (UNROLL * i + u)
                for t in range(2):
                    wait(v, "relu_ready", done + t + 1)
                    own.mark(nc.vector.tensor_tensor(mod[:, t], relu[:, t], relu[:, t], ALU.mult))
                for t in range(2):
                    lo = 4 * UNROLL * i + 4 * u + t
                    v.wait_ge(s_["hid_hi"], done + t + 1)
                    own.wait_back(1 - t)
                    nc.vector.tensor_tensor(big[:, lo], mod[:, t], big[:, lo + 2].bitcast(F32), ALU.subtract).then_inc(s_["hid_ready"], 1)

            def residual_chunk(name, i, u):
                kg = st[name].kg
                if u % kg == kg - 1:
                    gate = {"out": G_M, "m": G_F, "o": B0 + G_M, "n": B0 + G_F}[name if name in ("out", "o") else name[0]]
                    pair = (UNROLL // kg) * i + u // kg
                    v.wait_ge(s_["chunk_used"], st[name].m0 + UNROLL * i + u + 1)
                    for t in range(2):
                        k = 2 * pair + t
                        bank = BANK[2 * ((u // kg) % 2) + t]
                        nc.vector.scalar_tensor_tensor(out=xT[:, k], in0=bank[:, :], scalar=ada[:, gate + k], in1=xT[:, k],
                                                       op0=ALU.mult, op1=ALU.add).then_inc(s_["x_new"], 1)

            group_no = 1
            for name in ACTIVE:
                s = st[name]
                if name == "z":
                    step_sizes_vec(v, own)
                    scan_vec(v, own, split_next)
                    continue
                if name in ("kv", "q", "o"):
                    attention_vec(v, own, name, split_next, norm, residual_chunk)
                    continue
                if name in ("m1a", "n1a"):
                    b = name == "n1a"
                    norm(3 if b else 1, 4 if b else 1, 7 if b else 3, (B0 if b else 0) + SC_F)
                if s.lpc == 2:
                    ada_begin(group_no)

                def body(i, units):
                    for u in range(units):
                        if s.lpc == 2:
                            ada_step(s.l0 + 2 * u + 1, UNROLL * i + u, s.a0 + u, 2 * UNROLL, i)
                        split_next(name, i, u)
                        if name in ("x", "bc"):
                            conv_chunk(name, i, u)
                        elif name in HID0:
                            hidden_chunk(name, i, u)
                        else:
                            residual_chunk(name, i, u)

                links = {"x": 4, "bc": 4}.get(name, 2 if name in HID0 else 0) * UNROLL
                n = s.chunks // UNROLL
                if name in NEXT:
                    with v.Fori(0, n) as i:
                        own.enter(i, links)
                        body(i, UNROLL)
                    own.leave(n)
                else:
                    for i in range(n):
                        body(i, UNROLL)
                if s.lpc == 2:
                    ada_end(group_no, ADA[name][2])
                    group_no += 1
            for b in range(NCH):
                for q in range(2):
                    v.wait_ge(s_["out_t"], 2 * b + q + 1)
                    nc.vector.tensor_copy(fin[:, b, q * S:(q + 1) * S], BANK[(2 * b + q) % 4][:, :]).then_inc(s_["out_sb"], 1)

        @block.tensor
        def _(pe):
            def products(name, i, u, ks=range(KT), group=0, groups=1, ready=None):
                s = st[name]
                slot, hs = (s.l0 + s.lpc * u) % SLOTS, (s.m0 + u) % 2
                pair = (u // s.kg) % 2
                if ks[0] == 0:
                    pe.wait_ge(s_["lo_ready"], s.m0 + UNROLL * i + u + 1)
                for k in ks:
                    if ready:
                        ready(k)
                    if name in ("out", "m2a", "m2b", "n2a", "n2b"):
                        lo, hi = tile_at(KT * group + k)
                        xh, xl = big[:, hi], big[:, lo]
                    else:
                        xh, xl = h_hi[:, k], h_lo[:, k]
                    for t in range(2):
                        at_ = slice(k * CW + t * P, k * CW + (t + 1) * P)
                        dst = BANK[2 * pair + t][:, :]
                        first, final = (k == 0 and group == 0), (k == KT - 1 and group == groups - 1)
                        nc.tensor.matmul(dst, w_hi[:, hs, at_], xh, start=first, stop=False)
                        nc.tensor.matmul(dst, w_hi[:, hs, at_], xl, start=False, stop=False)
                        last = nc.tensor.matmul(dst, w_lo[:, slot, at_], xh, start=False, stop=final)
                return last

            def ada_reduce(n, used):
                pe.wait_ge(s_["ada_used"], used)
                if n:
                    pe.wait_ge(s_["ada_tab"], n)
                for j in range(2 * KT):
                    last = nc.tensor.matmul(MB[:, j:j + 1], acc[:, j * P:(j + 1) * P], ones[:, 0:1], start=True, stop=True)
                last.then_inc(s_["ada_sum"], 1)

            def norm(n):
                pe.wait_ge(s_["ss_done"], KT * (n + 1))
                nc.tensor.matmul(NB[:, :], ones[:, :], ssum[:, :], start=True, stop=True).then_inc(s_["ms_ready"], 1)

            pe.wait_ge(s_["consts"], 11)
            pe.wait_ge(s_["vec_in"], ROWS_IN)
            nc.tensor.transpose(MB[:, 0:120], pre[0:120, 0], ident[0:120, 0:120]).then_inc(s_["vec_t"], 1)
            nc.tensor.transpose(MB[:, P:2 * P], pre[:, 1], ident[:, :]).then_inc(s_["vec_t"], 1)
            nc.tensor.transpose(MB[:, 2 * P:2 * P + 54], pre[0:54, 2], ident[0:54, 0:54]).then_inc(s_["vec_t"], 1)
            for b in range(NCH):
                pe.wait_ge(x_loaded[b], 16)
            for k in range(KT):
                if k >= 4:
                    pe.wait_ge(s_["x_new"], k - 3)
                for b in range(NCH):
                    last = nc.tensor.transpose(BANK[k % 4][:, b * P:(b + 1) * P], x_in[:, b, k * P:(k + 1) * P], ident[:, :])
                last.then_inc(s_["xt_t"], 1)
            norm(0)
            ada_reduce(0, KT)

            def freed(name):
                if name in CONV0:
                    return "conv_sum", CONV0[name]
                if name in HID0:
                    return "relu_ready", HID0[name]
                return "x_new", X0[name]

            modulated = {"x": 0, "m1a": 1, "n1a": 4}
            before = ("x_new", KT)
            group_no = 1
            for name in ACTIVE:
                s = st[name]
                if name == "z":
                    step_sizes_pe(pe)
                    scan_pe(pe, products)
                    before = None
                    continue
                if name in ("kv", "q", "o"):
                    before = attention_pe(pe, name, products, norm, before)
                    continue
                if name in ("m1a", "n1a"):
                    norm(3 if name == "n1a" else 1)
                if before:
                    wait(pe, *before)
                elif name == "out":
                    wait(pe, "z_ready", 2 * GROUPS)
                    wait(pe, "groot_ready", GROUPS)
                sig, base = freed(name)

                def body(i, units):
                    for u in range(units):
                        pair = (UNROLL // s.kg) * i + u // s.kg
                        if u % s.kg == 0:
                            wait(pe, sig, base + 2 * (pair - 1))
                        if name in modulated and u == 0:
                            def ready(k):
                                pe.wait_ge(s_["h_ready"], KT * modulated[name] + k + 1)
                        elif name == "out" and u < 2:
                            def ready(k):
                                wait(pe, "y_out", KT * u + k + 1)
                        elif name[1:2] == "2" and u < 2:
                            def ready(k):
                                wait(pe, "hid_ready", HID0[name[0] + "1" + name[2]] + KT * u + k + 1)
                        else:
                            ready = None
                        products(name, i, u, group=u % s.kg, groups=s.kg, ready=ready).then_inc(s_["chunk_used"], 1)

                bodies(pe, name, body)
                if s.lpc == 2:
                    ada_reduce(group_no, s.a0 + s.chunks)
                    group_no += 1
                before = (sig, base + 2 * (s.chunks // s.kg))
            wait(pe, *before)
            for b in range(NCH):
                for q in range(2):
                    n = 2 * b + q
                    if n >= 4:
                        pe.wait_ge(s_["out_sb"], n - 3)
                    for j in range(4):
                        last = nc.tensor.transpose(BANK[n % 4][:, j * P:(j + 1) * P], xT[:, 4 * q + j, b * P:(b + 1) * P], ident[:, :])
                    last.then_inc(s_["out_t"], 1)


_INS = ["x", "c", "a_ada_w", "a_ada_b", "a_w_in", "a_conv_w", "a_conv_b", "a_dt_bias", "a_A_log", "a_D",
        "a_norm_w", "a_w_out", "a_mlp_w1", "a_mlp_w2", "kv_ada_w", "kv_ada_b", "kv_w", "k_norm",
        "b_ada_w", "b_ada_b", "b_w_q", "b_q_norm", "b_w_o", "b_mlp_w1", "b_mlp_w2"]


def kernel(**inputs):
    import numpy as np
    import concourse.bacc as bacc
    from concourse.bass_utils import run_bass_kernel_spmd

    nc = bacc.Bacc("TRN2", target_bir_lowering=False, num_devices=1)
    arrays, aps = {}, {}
    for name in _INS:
        a = np.ascontiguousarray(inputs[name])
        arrays["in_" + name] = a
        aps[name] = nc.dram_tensor("in_" + name, a.shape, mybir.dt.from_np(a.dtype), kind="ExternalInput").ap()
    out = nc.dram_tensor("out_x", (1, S, D), F32, kind="ExternalOutput").ap()
    trunk(nc, aps, out)
    r = run_bass_kernel_spmd(nc, [arrays], core_ids=[0])
    return r.results[0]["out_x"]
```

```python
import concourse.bass as bass
from concourse import mybir
from contextlib import ExitStack

F32 = mybir.dt.float32
F32R = mybir.dt.float32r
ALU = mybir.AluOpType
ACT = mybir.ActivationFunctionType
AX = mybir.AxisListType

P = 128
D = 1024
KT = D // P
S = 512
DI = 2 * D
GROUPS = 8
HEADS = 32
HPG = HEADS // GROUPS
NCH = 4
L = S // NCH
HD = 64
TAPS = 4
HID = 4 * D
NG = 3
QH = 16
KVH = 4
REP = QH // KVH
DIL = (1, 4, 16)
NEG = -1.0e30
EPS = 1e-6
GEPS = 1e-5
SLOTS = 4
CW = 256
UNROLL = 4


class Stage:

    def __init__(self, prev, chunks, lpc=1, kg=1):
        self.chunks, self.lpc, self.kg = chunks, lpc, kg
        self.m0 = prev.m0 + prev.chunks if prev else 0
        self.l0 = prev.l0 + prev.chunks * prev.lpc if prev else 0
        self.o0 = prev.o0 + prev.chunks // prev.kg if prev else 0
        self.a0 = prev.a0 + (prev.chunks if prev.lpc == 2 else 0) if prev else 0


class Chain:

    def __init__(self, eng, sem):
        self.eng, self.sem, self.n, self.i, self.per, self.start = eng, sem, 0, 0, 0, 0

    def mark(self, ins):
        ins.then_inc(self.sem, 1)
        self.n += 1

    def wait(self):
        self.eng.wait_ge(self.sem, self.i * self.per + self.n)

    def wait_back(self, n):
        self.eng.wait_ge(self.sem, self.i * self.per + self.n - n)

    def link(self, ins):
        self.mark(ins)
        self.wait()

    def enter(self, i, per):
        self.i, self.per, self.start = i, per, self.n

    def leave(self, times):
        assert self.n - self.start == self.per, (self.n - self.start, self.per)
        self.n += self.per * (times - 1)
        self.i = self.per = 0


def trunk(nc, ins, out):
    ctx = ExitStack()
    with ctx:
        cursor = [nc.sbuf_base + (-nc.sbuf_base) % 64]

        def sb(name, shape, dt=F32, at=None):
            size = 4
            for n in shape[1:]:
                size *= n
            if at is None:
                at = cursor[0]
                cursor[0] += size + (-size) % 64
                assert cursor[0] <= nc.sbuf_usable_end, (name, cursor[0])
            return nc.alloc_sbuf_tensor_at(name, shape, dt, offset=at), at

        def pb(name, shape):
            return ctx.enter_context(nc.psum_tensor(name, shape, F32))

        def sem(name):
            return ctx.enter_context(nc.semaphore(name))

        A0_LOADS = 8
        st = {}
        head = Stage(None, 0)
        head.l0, head.a0 = A0_LOADS, A0_LOADS
        order = [("x", 8, 2, 1), ("bc", 8, 2, 1), ("z", 8, 1, 1), ("out", 8, 1, 2),
                 ("m1a", 8, 2, 1), ("m2a", 8, 2, 2), ("m1b", 8, 2, 1), ("m2b", 8, 2, 2),
                 ("kv", 6, 1, 1), ("q", 12, 1, 1), ("o", 4, 1, 1),
                 ("n1a", 8, 1, 1), ("n2a", 8, 1, 2), ("n1b", 8, 1, 1), ("n2b", 8, 1, 2)]
        prev = head
        owner = {s: ("a", s) for s in range(A0_LOADS)}
        for name, chunks, lpc, kg in order:
            prev = st[name] = Stage(prev, chunks, lpc, kg)
            for j in range(chunks):
                owner[prev.l0 + lpc * j] = ("m", prev.m0 + j)
                if lpc == 2:
                    owner[prev.l0 + 2 * j + 1] = ("a", prev.a0 + j)

        def cols(w, n=CW):
            return w.rearrange("(k p) (n c) -> p n k c", p=P, c=n)

        w_in = ins["a_w_in"][0]
        wz = cols(w_in[:, 0:DI])
        wx = cols(w_in[:, DI:2 * DI])
        wbc = cols(w_in[:, 2 * DI:3 * DI])

        def tall(w, kg):
            return cols(w[kg * D:(kg + 1) * D, :])

        w_out = [tall(ins["a_w_out"][0], n) for n in range(2)]
        mlp = {}
        for tag, pre in (("m", "a"), ("n", "b")):
            mlp[tag + "1a"] = cols(ins[pre + "_mlp_w1"][0][:, 0:HID // 2])
            mlp[tag + "1b"] = cols(ins[pre + "_mlp_w1"][0][:, HID // 2:HID])
            mlp[tag + "2a"] = [tall(ins[pre + "_mlp_w2"][0], n) for n in range(2)]
            mlp[tag + "2b"] = [tall(ins[pre + "_mlp_w2"][0], n) for n in range(2, 4)]
        wkv = cols(ins["kv_w"])
        wq = cols(ins["b_w_q"][0])
        wo = cols(ins["b_w_o"][0])

        def main_src(name, i, u):
            if name in ("out",):
                return w_out[u % 2][:, 2 * i + u // 2]
            if name[1:2] == "2":
                return mlp[name][u % 2][:, 2 * i + u // 2]
            src = {"x": wx, "bc": wbc, "z": wz, "kv": wkv, "q": wq, "o": wo}.get(name)
            if src is None:
                src = mlp[name]
            return src[:, UNROLL * i + u]

        def ada_rows(w):
            return w.rearrange("(k p) (n c) -> p k n c", p=P, c=2 * D)

        ada_a, ada_b, ada_kv = ada_rows(ins["a_ada_w"][0]), ada_rows(ins["b_ada_w"][0]), ada_rows(ins["kv_ada_w"])
        ADA = {"x": (ada_a, 1, 16), "bc": (ada_a, 2, 32), "m1a": (ada_kv, 0, 96), "m2a": (ada_b, 0, 48),
               "m1b": (ada_b, 1, 64), "m2b": (ada_b, 2, 80)}
        SH_M, SC_M, G_M, SH_F, SC_F, G_F = range(0, 48, 8)
        KV_SH, KV_SC, B0 = 96, 104, 48

        xT, _ = sb("xT", [P, KT, S])
        h_hi, AT_H = sb("h_hi", [P, KT, S], F32R)
        h_lo, _ = sb("h_lo", [P, KT, S], F32R)
        conv, AT_BIG = sb("conv", [P, 4 * GROUPS, S])
        big, _ = sb("big", [P, 4 * GROUPS, S], F32R, at=AT_BIG)
        raw, AT_RAW = sb("raw", [P, SLOTS, KT * CW])
        w_lo, _ = sb("w_lo", [P, SLOTS, KT * CW], F32R, at=AT_RAW)
        w_hi, _ = sb("w_hi", [P, 2, KT * CW], F32R)
        ident, _ = sb("ident", [P, P])
        ones, _ = sb("ones", [P, P])
        tri, _ = sb("tri", [P, P])
        negm, _ = sb("negm", [P, P])
        vecs, _ = sb("vecs", [P, 120, 1])
        ada, _ = sb("ada", [P, 112, 1])
        taps, _ = sb("taps", [P, TAPS, HEADS, 1])
        vec2, _ = sb("vec2", [P, 54, 1])
        csil, _ = sb("csil", [P, KT, 1])
        dcol, _ = sb("dcol", [P, 2 * GROUPS, 1])
        dtab, _ = sb("dtab", [P, 4, NCH, GROUPS, HPG])
        half, _ = sb("half", [2, P])
        d_row, _ = sb("d_row", [2, 2 * GROUPS])
        dt_bias, _ = sb("dt_bias", [HEADS, 1])
        a_exp, _ = sb("a_exp", [P, HEADS])
        dt_w, _ = sb("dt_w", [P, KT, HEADS])
        credit, _ = sb("credit", [1, 64])
        MISC = cursor[0]

        def at(base, *shapes):
            found, p = [], base
            for shape in shapes:
                n = 4
                for x in shape:
                    n *= x
                found.append(p)
                p += n + (-n) % 64
            assert p <= nc.sbuf_usable_end, p
            return found

        o_acc, o_ss, o_sq, o_rt, o_rs, o_mod, o_r, = at(
            MISC, [2 * D], [S], [2, S], [S], [S], [2, S], [2, S])
        acc, _ = sb("acc", [P, 2 * D], at=o_acc)
        ssum, _ = sb("ssum", [P, S], at=o_ss)
        sq, _ = sb("sq", [P, 2, S], at=o_sq)
        root, _ = sb("root", [P, S], at=o_rt)
        rstd, _ = sb("rstd", [P, S], at=o_rs)
        mod, _ = sb("mod", [P, 2, S], at=o_mod)
        relu, _ = sb("relu", [P, 2, S], at=o_r)
        pre, _ = sb("pre", [P, 3, P], at=o_r)
        x_in, _ = sb("x_in", [P, NCH, D], at=AT_BIG)

        o_dh, o_dl, o_dT, o_v, o_e, o_z, o_zz, o_p, o_dA, o_cT = at(
            o_r + 4 * 2 * S, [KT, P], [KT, P], [S], [P], [P], [P], [P], [P], [P], [P])
        dtw_hi, _ = sb("dtw_hi", [P, KT, P], F32R, at=o_dh)
        dtw_lo, _ = sb("dtw_lo", [P, KT, P], F32R, at=o_dl)
        dt_T, _ = sb("dt_T", [HEADS, S], at=o_dT)
        sp_v, _ = sb("sp_v", [P, P], at=o_v)
        sp_e, _ = sb("sp_e", [P, P], at=o_e)
        sp_z, _ = sb("sp_z", [P, P], at=o_z)
        sp_zz, _ = sb("sp_zz", [P, P], at=o_zz)
        sp_p, _ = sb("sp_p", [P, P], at=o_p)
        dt_a, _ = sb("dt_a", [P, P], at=o_dA)
        cs_T, _ = sb("cs_T", [P, P], at=o_cT)
        cs_dram = nc.dram_tensor("cs_dram", (NCH, GROUPS, HPG, L), F32, kind="Internal").ap()

        (o_stg, o_ab, o_seg, o_xd, o_xe, o_bt, o_mt, o_s, o_st2, o_sz, o_gc, o_gq) = at(
            MISC, [4, S], [NCH, S], [2, S], [2, CW], [2, CW], [2, P], [2, S], [CW], [CW], [2, S],
            [2, 64], [2, S])
        stg, _ = sb("stg", [P, 4, S], at=o_stg)
        ab, _ = sb("ab", [P, NCH, HPG, L], at=o_ab)
        seg, _ = sb("seg", [P, 2, HPG, L], at=o_seg)
        x_dt, _ = sb("x_dt", [P, 2, HPG, HD], at=o_xd)
        x_end, _ = sb("x_end", [P, 2, HPG, HD], at=o_xe)
        b_tok, _ = sb("b_tok", [P, 2, P], at=o_bt)
        m_t, _ = sb("m_t", [P, 2, HPG, L], at=o_mt)
        state, _ = sb("state", [P, HPG, HD], at=o_s)
        s_dec, _ = sb("s_dec", [P, HPG, HD], at=o_st2)
        z_act, _ = sb("z_act", [P, 2, S], at=o_sz)
        gcol, _ = sb("gcol", [P, 2, 4, NCH, HPG, 1], at=o_gc)
        g_sq, _ = sb("g_sq", [P, 2, S], at=o_gq)
        fin, _ = sb("fin", [P, NCH, D], at=AT_BIG)

        PS = [pb(f"PS{n}", [P, S]) for n in range(8)]
        BANK = PS[0:4]
        NB, MB = PS[4], PS[5]

        raw_in = [sem(f"raw_in{n}") for n in range(SLOTS)]
        x_loaded = [sem(f"x_loaded{n}") for n in range(NCH)]
        ab_in = [sem(f"ab_in{n}") for n in range(NCH)]
        names = """vec_in pool_in consts vec_t vec_ok cs_ok xt_t x_new
            hi_ready lo_ready chunk_used ada_used ada_zero ada_sum ada_tab
            sq_ready ss_done ms_ready root_ready rstd_ready mod_ready h_hi_ready h_ready
            tap0 conv_sum conv_ready relu_ready hid_hi hid_ready dve_own act_own
            dtw_ready dt_ps dt_T_ready dt_t e_in e_ready dtA_ready aexp_ready cum_ready cs_sb dec_in dec_ready
            dtab_ready cs_T_ready cs_stored d_ps
            stg_ready cb_ready xdt_ready seg_ready lm_ready ecs_ready cs_ready mt_ready
            yps_ready st_ready state_ready y_ready z_ready yz_ready gsq_ready gsum_ready gms_ready
            groot_ready grstd_ready gmod_ready y_hi y_out
            masks_ready qk_sq qk_sum qk_root qk_rstd qk_done h_free v_perm v_tt v_tok qk_lo v_staged half_staged staged sc_ready masked max_ready neg_ready
            probs_ready pt_ps pt0_ready pt1_ready pv_ready o_kept stat_kept stat_t sum_t_ready below_top w_exp w_ready
            w_hi_ready w_split w_wide weighed mix_ab mixed o_hi o_ready out_t out_sb out_sem""".split()
        s_ = {n: sem(n) for n in names}

        X0 = {"init": 0, "out": 8, "m2a": 16, "m2b": 24, "o": 32, "n2a": 40, "n2b": 48}
        NORM_OF = {"init": 0, "out": 1, "m2b": 2, "o": 3}
        HID0 = {"m1a": 0, "m1b": 16, "n1a": 32, "n1b": 48}
        CREDIT = {"hid_ready": 2, "mt_ready": 2, "yps_ready": 2, "y_out": 1, "y_ready": 1, "z_ready": 3,
                  "groot_ready": 2, "cb_ready": 1, "cs_ready": 1, "state_ready": 1, "conv_sum": 3, "relu_ready": 3,
                  "masked": 2, "pt_ps": 2, "pt0_ready": 2, "pt1_ready": 1, "pv_ready": 5, "o_kept": 2, "stat_kept": 1, "staged": 1}
        POOL_IN, ROWS_IN = 16 * 4, 16 * 11
        CONV0 = {"x": 0, "bc": 16}
        block = ctx.enter_context(nc.Block())
        STAGES = [name for name, *_ in order]
        LAST = STAGES[-1]

        def tile_at(t):
            return 4 * (t // 2) + t % 2, 4 * (t // 2) + 2 + t % 2

        def bodies(eng, name, body):
            n = st[name].chunks // UNROLL
            if n > 1:
                with eng.Fori(0, n) as i:
                    body(i, UNROLL)
            elif n == 1:
                body(0, UNROLL)
            rest = st[name].chunks - n * UNROLL
            if rest:
                body(n, rest)

        def wait(eng, name, value):
            value = value + CREDIT.get(name, 0)
            eng.wait_ge(s_[name], value)
            if eng.engine in (nc.scalar.engine, nc.gpsimd.engine) and not isinstance(value, int):
                eng.nop(nofuse=True)

        def scan_pool(pool):
            pool.wait_ge(s_["dtab_ready"], 1)
            pool.wait_ge(s_["cs_T_ready"], 1)
            pool.dma_start(cs_dram.rearrange("c g h l -> (c g h) l"), cs_T[:, :]).then_inc(s_["cs_stored"], 16)
            pool.wait_ge(s_["cs_stored"], 16)

            def spread(c, g):
                pool.dma_start(ab[:, c], cs_dram[c, g].partition_broadcast(P)).then_inc(ab_in[c], 16)

            pool.wait_ge(s_["ada_tab"], 3)
            spread(0, 0)
            spread(1, 0)
            spread(2, 0)
            pool.wait_ge(s_["conv_ready"], 4 * GROUPS)

            def masked_sums(g, c):
                pool.wait_ge(ab_in[c], 16 * (g + 1))
                wait(pool, "mt_ready", NCH * g + c - 1)
                pool.tensor_tensor(seg[:, c % 2], ab[:, c],
                                   negm[:, :].unsqueeze(1).broadcast_to([P, HPG, L]), ALU.add).then_inc(s_["seg_ready"], 1)

            def group(g):
                final = isinstance(g, int) and g == GROUPS - 1
                for c in range(NCH):
                    it = NCH * g + c
                    if c < NCH - 1:
                        masked_sums(g, c + 1)
                    elif not final:
                        masked_sums(g + 1, 0)
                    if c:
                        n = (NCH - 1) * g + c
                        pool.wait_ge(s_["ecs_ready"], n)
                        pool.tensor_tensor(ab[:, c], ab[:, c],
                                           conv[:, 4 * g + 3, c * L:(c + 1) * L].unsqueeze(1).broadcast_to([P, HPG, L]),
                                           ALU.mult).then_inc(s_["cs_ready"], 1)
                    wait(pool, "yps_ready", it)
                    if c == 0:
                        spread(NCH - 1, g)
                    elif not final:
                        spread(c - 1, g + 1)

            masked_sums(0, 0)
            with pool.Fori(0, GROUPS - 1) as g:
                group(g)
            group(GROUPS - 1)


        def conv_tile(name, i, u, t):
            if name == "x":
                return 2 * UNROLL * i + 2 * u + t, 4 * UNROLL * i + 4 * u + t
            return 2 * GROUPS + 2 * UNROLL * i + 2 * u + t, i + 4 * (2 * u + t) + 2

        def step_sizes_act(act, chunk):
            if chunk == 1:
                wait(act, "dt_ps", 1)
                wait(act, "pool_in", POOL_IN)
                nc.scalar.activation(dt_T[:, :], PS[6][0:HEADS, :], ACT.Identity, bias=dt_bias[:, 0:1]).then_inc(s_["dt_T_ready"], 1)
            elif chunk == 2:
                nc.scalar.activation(a_exp[:, :], a_exp[:, :], ACT.Exp).then_inc(s_["aexp_ready"], 1)
                wait(act, "e_in", 1)
                nc.scalar.activation(sp_e[:, :], sp_p[:, :], ACT.Exp, scale=-1.0).then_inc(s_["e_ready"], 1)
            elif chunk == 5:
                wait(act, "dec_in", 1)
                nc.scalar.activation(sp_e[:, :], sp_z[:, :], ACT.Exp).then_inc(s_["dec_ready"], 1)
                nc.scalar.activation(dtab[:, 3].rearrange("p c g h -> p (c g h)"), sp_zz[:, :], ACT.Exp).then_inc(s_["dec_ready"], 1)

        def step_sizes_vec(v, own, chunk):
            flat = dtab[:, :, :, :, :].rearrange("p k c g h -> p k (c g h)")
            if chunk == 0:
                v.wait_ge(s_["pool_in"], POOL_IN)
                own.mark(nc.vector.memset(dtw_hi[:, :, :].bitcast(F32), 0.0))
                own.link(nc.vector.memset(dtw_lo[:, :, :].bitcast(F32), 0.0))
                own.link(nc.vector.tensor_copy(dtw_hi[:, :, 0:HEADS], dt_w[:, :, :]))
                nc.vector.tensor_tensor(dtw_lo[:, :, 0:HEADS], dt_w[:, :, :], dtw_hi[:, :, 0:HEADS].bitcast(F32),
                                        ALU.subtract).then_inc(s_["dtw_ready"], 1)
            elif chunk == 2:
                v.wait_ge(s_["dt_t"], 1)
                own.link(nc.vector.tensor_copy(sp_v[:, :], PS[7][:, 0:P]))
                nc.vector.scalar_tensor_tensor(out=sp_p[:, :], in0=sp_v[:, :], scalar=-1.0, in1=sp_v[:, :],
                                               op0=ALU.mult, op1=ALU.max).then_inc(s_["e_in"], 1)
            elif chunk == 3:
                v.wait_ge(s_["e_ready"], 1)
                own.link(nc.vector.tensor_scalar(sp_z[:, :], sp_e[:, :], 2.0, None, ALU.add))
                own.link(nc.vector.reciprocal(sp_z[:, :], sp_z[:, :]))
                own.link(nc.vector.tensor_tensor(sp_z[:, :], sp_z[:, :], sp_e[:, :], ALU.mult))
                own.link(nc.vector.tensor_tensor(sp_zz[:, :], sp_z[:, :], sp_z[:, :], ALU.mult))
                own.link(nc.vector.tensor_scalar(sp_p[:, :], sp_zz[:, :], 1.0 / 15, None, ALU.mult))
                for n in (13, 11, 9, 7, 5, 3):
                    own.link(nc.vector.scalar_tensor_tensor(out=sp_p[:, :], in0=sp_p[:, :], scalar=1.0 / n, in1=sp_zz[:, :],
                                                            op0=ALU.add, op1=ALU.mult))
                own.link(nc.vector.scalar_tensor_tensor(out=sp_p[:, :], in0=sp_p[:, :], scalar=1.0, in1=sp_z[:, :],
                                                        op0=ALU.add, op1=ALU.mult))
                own.link(nc.vector.tensor_scalar(sp_v[:, :], sp_v[:, :], 0.0, None, ALU.max))
                own.link(nc.vector.scalar_tensor_tensor(out=flat[:, 0], in0=sp_p[:, :], scalar=2.0, in1=sp_v[:, :],
                                                        op0=ALU.mult, op1=ALU.add))
                v.wait_ge(s_["aexp_ready"], 1)
                nc.vector.scalar_tensor_tensor(out=dt_a[:, :].rearrange("p (c h) -> p c h", c=NCH),
                                               in0=flat[:, 0].rearrange("p (c h) -> p c h", c=NCH), scalar=-1.0,
                                               in1=a_exp[:, :].unsqueeze(1).broadcast_to([P, NCH, HEADS]),
                                               op0=ALU.mult, op1=ALU.mult).then_inc(s_["dtA_ready"], 1)
            elif chunk == 5:
                v.wait_ge(s_["cum_ready"], 1)
                nc.vector.tensor_copy(sp_v[:, :], PS[7][:, P:2 * P]).then_inc(s_["cs_sb"], 1)
                own.link(nc.vector.tensor_scalar(flat[:, 1], PS[7][:, P:2 * P], -1.0, None, ALU.mult))
                own.link(nc.vector.tensor_copy(sp_zz[:, :], PS[7][:, 2 * P:3 * P]))
                nc.vector.tensor_tensor(sp_z[:, :], sp_zz[:, :], flat[:, 1], ALU.add).then_inc(s_["dec_in"], 1)
            elif chunk == 7:
                v.wait_ge(s_["d_ps"], 1)
                nc.vector.tensor_copy(cs_T[:, :], PS[6][:, 0:P]).then_inc(s_["cs_T_ready"], 1)
                own.link(nc.vector.tensor_copy(dcol[:, :, 0], PS[6][:, P:P + 2 * GROUPS]))
                v.wait_ge(s_["dec_ready"], 2)
                nc.vector.tensor_tensor(flat[:, 2], flat[:, 0], sp_e[:, :], ALU.mult).then_inc(s_["dtab_ready"], 1)

        def step_sizes_pe(pe, chunk):
            if chunk == 1:
                pe.wait_ge(s_["dtw_ready"], 1)
                for k in range(KT):
                    for w, x in ((dtw_hi, h_hi), (dtw_hi, h_lo), (dtw_lo, h_hi)):
                        last = nc.tensor.matmul(PS[6][:, :], w[:, k], x[:, k], start=(k == 0 and w is dtw_hi and x is h_hi),
                                                stop=(k == KT - 1 and w is dtw_lo))
                last.then_inc(s_["dt_ps"], 1)
            elif chunk == 2:
                pe.wait_ge(s_["dt_T_ready"], 1)
                for c in range(NCH):
                    last = nc.tensor.transpose(PS[7][:, c * HEADS:(c + 1) * HEADS], dt_T[:, c * L:(c + 1) * L], ident[0:HEADS, 0:HEADS])
                last.then_inc(s_["dt_t"], 1)
            elif chunk == 5:
                pe.wait_ge(s_["dtA_ready"], 1)
                nc.tensor.matmul(PS[7][:, P:2 * P], tri[:, :], dt_a[:, :], start=True, stop=True)
                nc.tensor.matmul(PS[7][:, 2 * P:3 * P], ones[:, :], dt_a[:, :], start=True, stop=True).then_inc(s_["cum_ready"], 1)
            elif chunk == 7:
                pe.wait_ge(s_["cs_sb"], 1)
                pe.wait_ge(s_["pool_in"], POOL_IN)
                nc.tensor.transpose(PS[6][:, 0:P], sp_v[:, :], ident[:, :])
                nc.tensor.matmul(PS[6][:, P:P + 2 * GROUPS], half[:, :], d_row[:, :], start=True, stop=True).then_inc(s_["d_ps"], 1)

        def lag_act(act, g, gp, c):
            if c == 1:
                for t in range(2):
                    wait(act, "yz_ready", 2 * g + t + 1)
                    nc.scalar.activation(g_sq[:, t], conv[:, 4 * g + t], ACT.Square).then_inc(s_["gsq_ready"], 1)
            if c == 2:
                wait(act, "gms_ready", g + 1)
                nc.scalar.activation(g_sq[:, 1], BANK[2 * gp][:, :], ACT.Ln, bias=GEPS, scale=1.0 / CW).then_inc(s_["groot_ready"], 1)
                wait(act, "groot_ready", g + 1)
                nc.scalar.activation(g_sq[:, 0], g_sq[:, 1], ACT.Exp, scale=-0.5).then_inc(s_["grstd_ready"], 1)
            if c == 3:
                for t in range(2):
                    wait(act, "gmod_ready", 2 * g + t + 1)
                    nc.scalar.activation(big[:, 4 * g + 2 + t], z_act[:, t], ACT.Copy).then_inc(s_["y_hi"], 1)

        def steps_of(units):
            steps = [(u, c) for u in range(units) for c in range(NCH)]
            return list(zip(steps, steps[1:] + [None]))

        def scan_act(act, split_next):
            def body(i, units):
                def decays(u, c):
                    g, gp = UNROLL * i + u, u % 2
                    wait(act, "stg_ready", g + 1)
                    wait(act, "seg_ready", NCH * g + c + 1)
                    for hh in range(HPG):
                        last = nc.scalar.activation(seg[:, c % 2, hh], seg[:, c % 2, hh], ACT.Exp, bias=gcol[:, gp, 1, c, hh])
                    last.then_inc(s_["lm_ready"], 1)
                    if c:
                        nc.scalar.activation(ab[:, c], ab[:, c], ACT.Exp).then_inc(s_["ecs_ready"], 1)

                def gate(g):
                    wait(act, "chunk_used", st["z"].m0 + g + 1)
                    wait(act, "y_out", 2 * g)
                    for t in range(2):
                        nc.scalar.activation(z_act[:, t], BANK[2 * (g % 2) + t][:, :], ACT.Silu).then_inc(s_["z_ready"], 1)

                decays(0, 0)
                for (u, c), after in steps_of(units):
                    g, gp = UNROLL * i + u, u % 2
                    if after:
                        decays(*after)
                    if c == 0 and u:
                        gate(g - 1)
                    if c == 1:
                        split_next("z", i, u)
                    if u:
                        lag_act(act, g - 1, 1 - gp, c)
                gate(GROUPS - 1)
                for c in range(NCH):
                    lag_act(act, GROUPS - 1, 1, c)

            body(0, GROUPS)

        def lag_vec(v, g, gp, c):
            if c == 0:
                wait(v, "y_ready", NCH * g + NCH)
                for t in range(2):
                    wait(v, "z_ready", 2 * g + t + 1)
                    nc.vector.tensor_tensor(conv[:, 4 * g + t], conv[:, 4 * g + t], z_act[:, t], ALU.mult).then_inc(s_["yz_ready"], 1)
            if c == 1:
                v.wait_ge(s_["gsq_ready"], 2 * g + 2)
                nc.vector.tensor_tensor(g_sq[:, 0], g_sq[:, 0], g_sq[:, 1], ALU.add).then_inc(s_["gsum_ready"], 1)
            if c == 3:
                for t in range(2):
                    v.wait_ge(s_["y_hi"], 2 * g + t + 1)
                    nc.vector.tensor_tensor(big[:, 4 * g + t], z_act[:, t], big[:, 4 * g + 2 + t].bitcast(F32),
                                            ALU.subtract).then_inc(s_["y_out"], 1)

        def scale_vec(v, g):
            v.wait_ge(s_["grstd_ready"], g + 1)
            for t in range(2):
                nc.vector.scalar_tensor_tensor(out=z_act[:, t], in0=conv[:, 4 * g + t], scalar=vec2[:, 32 + 2 * g + t],
                                               in1=g_sq[:, 0], op0=ALU.mult, op1=ALU.mult).then_inc(s_["gmod_ready"], 1)

        def scan_vec(v, own, split_lo_next):
            v.wait_ge(s_["conv_ready"], 4 * GROUPS)
            v.wait_ge(s_["dtab_ready"], 1)
            conv_g = conv[:, :, :].rearrange("p (g f) s -> p g f s", f=4)

            def col(gp, kind, c, n):
                return gcol[:, gp, kind, c].broadcast_to([P, HPG, n])

            def body(i, units):
                def stage_group(u):
                    g = UNROLL * i + u
                    wait(v, "cb_ready", NCH * g)
                    own.mark(nc.vector.tensor_copy(gcol[:, u % 2, :, :, :, 0], dtab[:, :, :, g]))
                    nc.vector.tensor_copy(stg[:, :, :], conv_g[:, g]).then_inc(s_["stg_ready"], 1)
                    own.wait()

                def operands(u, c):
                    it = NCH * (UNROLL * i + u) + c
                    tb, cp, gp = PS[4 + c % 2], c % 2, u % 2
                    x_tok = tb[:, 0:CW].rearrange("p (h d) -> p h d", h=HPG)
                    wait(v, "cb_ready", it + 1)
                    last = nc.vector.tensor_tensor(x_dt[:, cp], x_tok, col(gp, 0, c, HD), ALU.mult)
                    if c < NCH - 1:
                        nc.vector.tensor_tensor(x_end[:, cp], x_tok, col(gp, 2, c, HD), ALU.mult)
                        last = nc.vector.tensor_copy(b_tok[:, cp], tb[:, CW:CW + P])
                    last.then_inc(s_["xdt_ready"], 1)
                    v.wait_ge(s_["lm_ready"], it + 1)
                    nc.vector.tensor_tensor(m_t[:, cp], tb[:, 3 * P:4 * P].unsqueeze(1).broadcast_to([P, HPG, L]),
                                            seg[:, cp], ALU.mult).then_inc(s_["mt_ready"], 1)

                stage_group(0)
                operands(0, 0)
                for (u, c), after in steps_of(units):
                    g, gp = UNROLL * i + u, u % 2
                    it = NCH * g + c
                    if after and c:
                        if after[1] == 0:
                            stage_group(u + 1)
                        operands(*after)
                    if c == NCH - 1 and u:
                        scale_vec(v, g - 1)
                    wait(v, "yps_ready", it + 1)
                    for j in range(2):
                        y_t = conv[:, 4 * g + j, c * L:(c + 1) * L]
                        last = nc.vector.scalar_tensor_tensor(out=y_t, in0=y_t, scalar=dcol[:, 2 * g + j],
                                                              in1=PS[6][:, j * L:(j + 1) * L], op0=ALU.mult, op1=ALU.add)
                    last.then_inc(s_["y_ready"], 1)
                    if c < NCH - 1:
                        new = PS[7][:, 0:CW].rearrange("p (h d) -> p h d", h=HPG)
                        if c:
                            own.link(nc.vector.tensor_tensor(s_dec[:, :, :], state[:, :, :], col(gp, 3, c, HD), ALU.mult))
                            v.wait_ge(s_["st_ready"], (NCH - 1) * g + c + 1)
                            last = nc.vector.tensor_tensor(state[:, :, :], s_dec[:, :, :], new, ALU.add)
                        else:
                            v.wait_ge(s_["st_ready"], (NCH - 1) * g + c + 1)
                            last = nc.vector.tensor_copy(state[:, :, :], new)
                        last.then_inc(s_["state_ready"], 1)
                        wait(v, "state_ready", (NCH - 1) * g + c + 1)
                    if c == 0:
                        operands(*after)
                    if c == 1:
                        split_lo_next("z", i, u)
                    if u:
                        lag_vec(v, g - 1, 1 - gp, c)
                for c in range(NCH):
                    if c == NCH - 1:
                        scale_vec(v, GROUPS - 1)
                    lag_vec(v, GROUPS - 1, 1, c)

            body(0, GROUPS)

        def scan_pe(pe, products):
            wait(pe, "conv_sum", 4 * GROUPS)

            def group_sum(g, gp):
                pe.wait_ge(s_["gsum_ready"], g + 1)
                wait(pe, "z_ready", 2 * g + 2)
                nc.tensor.matmul(BANK[2 * gp][:, :], ones[:, :], g_sq[:, 0], start=True, stop=True).then_inc(s_["gms_ready"], 1)

            def body(i, units):
                def by_tokens(u, c):
                    g = UNROLL * i + u
                    tb, sl = PS[4 + c % 2], slice(c * L, (c + 1) * L)
                    pe.wait_ge(s_["stg_ready"], g + 1)
                    wait(pe, "mt_ready", NCH * g + c - 1)
                    for j in range(3 if c < NCH - 1 else 2):
                        nc.tensor.transpose(tb[:, j * P:(j + 1) * P], stg[:, j, sl], ident[:, :])
                    nc.tensor.matmul(tb[:, 3 * P:4 * P], stg[:, 2, sl], stg[:, 3, sl], start=True, stop=True).then_inc(s_["cb_ready"], 1)

                by_tokens(0, 0)
                for (u, c), after in steps_of(units):
                    g, gp = UNROLL * i + u, u % 2
                    it, cp = NCH * g + c, c % 2
                    if c == 0:
                        wait(pe, "z_ready", 2 * g - 2)
                        wait(pe, "groot_ready", g - 1)
                    last = products("z", i, u, range(2 * c, 2 * c + 2))
                    if c == NCH - 1:
                        last.then_inc(s_["chunk_used"], 1)
                    if after:
                        by_tokens(*after)
                    if c == 2 and u:
                        group_sum(g - 1, 1 - gp)
                    pe.wait_ge(s_["xdt_ready"], it + 1)
                    wait(pe, "mt_ready", it + 1)
                    wait(pe, "y_ready", it)
                    if c:
                        wait(pe, "cs_ready", (NCH - 1) * g + c)
                        wait(pe, "state_ready", (NCH - 1) * g + c)
                    for hh in range(HPG):
                        dst = PS[6][HD * (hh % 2):HD * (hh % 2) + HD, (hh // 2) * L:(hh // 2 + 1) * L]
                        last = nc.tensor.matmul(dst, x_dt[:, cp, hh], m_t[:, cp, hh], start=True, stop=(c == 0))
                        if c:
                            last = nc.tensor.matmul(dst, state[:, hh], ab[:, c, hh], start=False, stop=True)
                    last.then_inc(s_["yps_ready"], 1)
                    if c < NCH - 1:
                        wait(pe, "state_ready", (NCH - 1) * g + c)
                        nc.tensor.matmul(PS[7][:, 0:CW], b_tok[:, cp], x_end[:, cp].rearrange("p h d -> p (h d)"),
                                         start=True, stop=True).then_inc(s_["st_ready"], 1)
            body(0, GROUPS)
            return lambda: group_sum(GROUPS - 1, 1)

        KV_END, Q_END = st["kv"].m0 + st["kv"].chunks, st["q"].m0 + st["q"].chunks
        K_TILES = NG * KVH // 2
        UNITS = NG * KVH
        BLOCKS = S // P
        BODY = 2 * BLOCKS
        q_all, _ = sb("q_all", [P, NG * QH // 2, S], at=AT_BIG)
        k_all, _ = sb("k_all", [P, K_TILES, S], at=AT_BIG + 4 * S * NG * QH // 2)
        o_sqk, o_vp = at(o_acc, [2, S], [2, S])
        qk_sq_lo, _ = sb("qk_sq_lo", [P, 2, S], F32R, at=o_sqk)
        qk_sq_hi, _ = sb("qk_sq_hi", [P, 2, S], F32R, at=o_vp)
        qk_s, _ = sb("qk_s", [P, 2, S], at=o_sqk)
        v_order, _ = sb("v_order", [P, 2, S], at=o_vp)
        (o_vt,) = at(o_r + 4 * 2 * S, [NG, BLOCKS, KVH * HD])
        v_all, _ = sb("v_all", [P, NG, BLOCKS, KVH * HD], at=o_vt)
        o_mk, o_mr, o_bd = at(o_vt + 4 * NG * BLOCKS * KVH * HD, [2, P], [P], [P])
        win_mask, _ = sb("win_mask", [P, 2, P], at=o_mk)
        res_mask, _ = sb("res_mask", [P, P], at=o_mr)
        head_ones, _ = sb("head_ones", [P, P], F32R, at=o_bd)
        head_row, _ = sb("head_row", [QH, QH // 2, P], F32R, at=o_r)
        o_qs, o_sm, o_pt = at(AT_H, [2, 2, S], [2, REP, 2 * P], [2, 2, S])
        q_u, _ = sb("q_u", [P, 2, 2, S], at=o_qs)
        k_u, _ = sb("k_u", [P, 2, S], at=o_mod)
        v_u, _ = sb("v_u", [P, 2, BLOCKS, HD], at=o_rs)
        probs, _ = sb("probs", [P, 2, REP, 2 * P], at=o_sm)
        probs_t, _ = sb("probs_t", [P, 2, 2, REP, P], at=o_pt)
        o_b1, o_b2, o_b3, o_b4 = at(o_acc, [2, 2, BLOCKS, REP], [2, BLOCKS, REP], [NG, BLOCKS, KVH, REP], [NG, BLOCKS, KVH, REP])
        stat, _ = sb("stat", [P, 2, 2, BLOCKS, REP], at=o_b1)
        neg_max, _ = sb("neg_max", [P, 2, BLOCKS, REP, 1], at=o_b2)
        max_all, _ = sb("max_all", [P, NG, BLOCKS, KVH, REP], at=o_b3)
        sum_all, _ = sb("sum_all", [P, NG, BLOCKS, KVH, REP], at=o_b4)
        o_c1, o_c2, o_c3 = at(AT_BIG + 4 * S * NG * QH // 2, [NG, S], [NG, S], [S])
        w_t, _ = sb("w_t", [QH, NG, S], at=o_c1)
        sum_t, _ = sb("sum_t", [QH, NG, S], at=o_c2)
        top, _ = sb("top", [QH, S], at=o_c3)
        mix_a, _ = sb("mix_a", [P, 2, S], at=o_sqk)
        mix_b, _ = sb("mix_b", [P, 2, S], at=o_vp)
        mix_c, _ = sb("mix_c", [P, 2, S], at=o_mod)
        w_t_hi, _ = sb("w_t_hi", [QH, NG, S], F32R, at=o_c2)
        w_t_lo, _ = sb("w_t_lo", [QH, NG, S], F32R, at=o_c1)

        def by_residue(ap, g):
            return ap.rearrange("p (i r) -> p r i", r=DIL[g])

        def in_residues(ap, g):
            return ap.rearrange("p (r i) -> p r i", r=DIL[g])

        def attention_masks(pool):
            own = s_["masks_ready"]
            wait(pool, "hid_ready", 2 * st["m1a"].chunks + 2 * st["m1b"].chunks)
            wait(pool, "ada_tab", 7)
            pool.memset(win_mask[:, 1], 0.0).then_inc(own, 1)
            pool.memset(head_ones[:, :].bitcast(F32), 1.0).then_inc(own, 1)
            pool.memset(head_row[:, :, :].bitcast(F32), 1.0).then_inc(own, 1)
            pool.tensor_copy(win_mask[:, 0], negm[:, :]).then_inc(own, 1)
            pool.wait_ge(own, 4)
            pool.affine_select(out=win_mask[:, 1], in_=win_mask[:, 1], compare_op=ALU.is_ge, fill=NEG, base=0,
                               pattern=[[-1, P]], channel_multiplier=1).then_inc(own, 1)
            pool.affine_select(out=head_ones[:, :], in_=head_ones[:, :].bitcast(F32), compare_op=ALU.is_ge, fill=0.0, base=0,
                               pattern=[[-HD, 2], [0, HD]], channel_multiplier=1).then_inc(own, 1)
            pool.affine_select(out=head_row[:, :, :], in_=head_row[:, :, :].bitcast(F32), compare_op=ALU.is_ge, fill=0.0, base=0,
                               pattern=[[P, QH // 2], [1, P]], channel_multiplier=-HD).then_inc(own, 1)
            pool.wait_ge(own, 7)
            pool.affine_select(out=res_mask[:, :], in_=win_mask[:, 1], compare_op=ALU.is_ge, fill=NEG, base=S // DIL[2] - 1,
                               pattern=[[S // DIL[2], P * DIL[2] // S], [0, S // DIL[2]]], channel_multiplier=-1).then_inc(own, 1)
            pool.affine_select(out=head_ones[:, :], in_=head_ones[:, :].bitcast(F32), compare_op=ALU.is_ge, fill=0.0, base=HD - 1,
                               pattern=[[HD, 2], [0, HD]], channel_multiplier=-1).then_inc(own, 1)
            pool.affine_select(out=head_row[:, :, :], in_=head_row[:, :, :].bitcast(F32), compare_op=ALU.is_ge, fill=0.0, base=HD - 1,
                               pattern=[[-P, QH // 2], [-1, P]], channel_multiplier=HD).then_inc(own, 1)

        def attention_pool(pool):
            pool.wait_ge(s_["qk_done"], K_TILES)
            pool.wait_ge(s_["v_tok"], K_TILES)
            pool.wait_ge(s_["h_ready"], KT * 4)
            for g in range(NG):
                with pool.Fori(0, KVH // 2) as i:
                    for u in range(2):
                        unit = KVH * g + 2 * i + u
                        wait(pool, "pv_ready", BLOCKS * (unit - 1))
                        wait(pool, "staged", unit)
                        for side in range(2):
                            pool.tensor_copy(k_u[side * HD:(side + 1) * HD, u],
                                             k_all[u * HD:(u + 1) * HD, 2 * g + i]).then_inc(s_["half_staged"], 1)
                            wait(pool, "half_staged", 2 * unit + side + 1)
                        pool.tensor_copy(v_u[:, u], v_all[:, g, :, :].rearrange("p b (i h d) -> p b i h d", i=2, h=2)[:, :, i, u]).then_inc(s_["v_staged"], 1)
                        pool.wait_ge(s_["chunk_used"], Q_END)
                        pool.wait_ge(s_["qk_done"], K_TILES + NG * QH // 2)
                        wait(pool, "v_staged", unit + 1)
                        for j in range(2):
                            last = pool.tensor_copy(in_residues(q_u[:, u, j], g),
                                                    by_residue(q_all[:, KT * g + 4 * i + 2 * u + j], g))
                        last.then_inc(s_["staged"], 1)
            for k in range(KT):
                pool.wait_ge(s_["weighed"], k + 1)
                pool.tensor_tensor(mix_a[:, k % 2], mix_a[:, k % 2], mix_b[:, k % 2], ALU.add).then_inc(s_["mix_ab"], 1)
                pool.wait_ge(s_["mix_ab"], k + 1)
                pool.tensor_tensor(mix_a[:, k % 2], mix_a[:, k % 2], mix_c[:, k % 2], ALU.add).then_inc(s_["mixed"], 1)

        def norm_act(act, done, scale, bias):
            for t in range(2):
                wait(act, "qk_sum", done + t + 1)
                nc.scalar.activation(qk_s[:, t], PS[6 + t][:, :], ACT.Ln, bias=bias, scale=scale).then_inc(s_["qk_root"], 1)
            for t in range(2):
                wait(act, "qk_root", done + t + 1)
                nc.scalar.activation(qk_s[:, t], qk_s[:, t], ACT.Exp, scale=-0.5).then_inc(s_["qk_rstd"], 1)

        def norm_vec(v, done, pair, cols_, dests):
            for t in range(2):
                v.wait_ge(s_["qk_rstd"], done + t + 1)
                dst, src, rs = dests(t), BANK[2 * pair + t][:, :], qk_s[:, t]
                if len(dst.shape) == 3:
                    src, rs = by_residue(src, cols_[1]), by_residue(rs, cols_[1])
                nc.vector.scalar_tensor_tensor(out=dst, in0=src, scalar=vec2[:, cols_[0]], in1=rs,
                                               op0=ALU.mult, op1=ALU.mult).then_inc(s_["qk_done"], 1)

        def squares_vec(v, done):
            for t in range(2):
                v.wait_ge(s_["qk_sq"], 2 * (done + t + 1))
                nc.vector.tensor_tensor(qk_sq_lo[:, t], qk_s[:, t], qk_sq_hi[:, t].bitcast(F32), ALU.subtract).then_inc(s_["qk_lo"], 1)

        def sums_pe(pe, done, first=False):
            for t in range(2):
                pe.wait_ge(s_["qk_lo"], done + t + 1)
                if not first:
                    pe.wait_ge(s_["qk_root"], done + t - 1)
                nc.tensor.matmul(PS[6 + t][:, :], head_ones[:, :], qk_sq_hi[:, t], start=True, stop=False)
                nc.tensor.matmul(PS[6 + t][:, :], head_ones[:, :], qk_sq_lo[:, t], start=False, stop=True).then_inc(s_["qk_sum"], 1)

        def blocks_of(g):
            return [(n, n // BLOCKS, n % BLOCKS, 2 if g == 0 and n % BLOCKS else 1) for n in range(BODY)]

        def attention_act(act, name, split_next, norm, residual_chunk):
            if name == "kv":
                norm(2, 2, st["m1b"].m0 + st["m1b"].chunks, 4, KV_SH)
                wait(act, "ada_tab", 7)
                for j in range(st["kv"].chunks):
                    i, u = divmod(j, UNROLL)
                    split_next("kv", i, u)
                    if 0 < j <= K_TILES // 2:
                        norm_act(act, 2 * (j - 1), 1.0 / HD, EPS)
                    if j == st["kv"].chunks - 1:
                        norm(None, 3, None, 5, B0 + SH_M)
                    m = st["kv"].m0 + j
                    wait(act, "chunk_used", m + 1)
                    for t in range(2):
                        bank = BANK[2 * (j % 2) + t][:, :]
                        if j < K_TILES // 2:
                            if j:
                                wait(act, "qk_done", 2 * j - 1 + t)
                            for sq_ in (qk_s, qk_sq_hi):
                                nc.scalar.activation(sq_[:, t], bank, ACT.Square).then_inc(s_["qk_sq"], 1)
                        else:
                            n = 2 * j - K_TILES + t
                            if n >= 2:
                                wait(act, "v_tt", n - 1)
                            g = n // 2
                            nc.scalar.activation(in_residues(v_order[:, t], g), by_residue(bank, g), ACT.Copy).then_inc(s_["v_perm"], 1)
            elif name == "q":
                wait(act, "v_tt", K_TILES)
                with act.Fori(0, NG) as i:
                    for u in range(UNROLL):
                        c = UNROLL * i + u
                        split_next("q", i, u)
                        if u:
                            norm_act(act, K_TILES + 2 * (c - 1), 1.0, HD * EPS)
                        wait(act, "chunk_used", st["q"].m0 + c + 1)
                        for t in range(2):
                            wait(act, "qk_done", K_TILES + 2 * c - 1 + t)
                            for sq_ in (qk_s, qk_sq_hi):
                                nc.scalar.activation(sq_[:, t], BANK[2 * (u % 2) + t][:, :], ACT.Square).then_inc(s_["qk_sq"], 1)
                    norm_act(act, K_TILES + 2 * (UNROLL * i + UNROLL - 1), 1.0, HD * EPS)
            else:
                wait(act, "qk_done", K_TILES + NG * QH // 2)
                for g in range(NG):
                    with act.Fori(0, 2) as i:
                        base = BODY * (2 * g + i)
                        blocks = blocks_of(g)
                        wait(act, "stat_kept", 2 * g + i)
                        for step in range(BODY + 1):
                            if step < BODY:
                                n, u, b, nk = blocks[step]
                                wait(act, "neg_ready", base + n + 1)
                                for r in range(REP):
                                    last = nc.scalar.activation(probs[:, n % 2, r, 0:nk * P], probs[:, n % 2, r, 0:nk * P], ACT.Exp,
                                                                bias=neg_max[:, u, b, r], accum_out=stat[:, 1, u, b, r:r + 1])
                                last.then_inc(s_["probs_ready"], 1)
                            if step:
                                n, u, b, nk = blocks[step - 1]
                                wait(act, "pt_ps", base + n + 1)
                                wait(act, "pv_ready", base + n - 1)
                                nc.scalar.activation(probs_t[:, n % 2, 0].rearrange("p r q -> p (r q)"), PS[4 + n % 2][:, :],
                                                     ACT.Copy).then_inc(s_["pt0_ready"], 1)
                for g in range(NG):
                    act.wait_ge(s_["stat_t"], 2 * g + 2)
                    nc.scalar.activation(by_residue(sum_t[:, g], g), in_residues(PS[2 * g + 1][0:QH, :], g), ACT.Copy).then_inc(s_["sum_t_ready"], 1)
                for g in range(NG):
                    act.wait_ge(s_["below_top"], g + 1)
                    nc.scalar.activation(w_t[:, g], w_t[:, g], ACT.Exp).then_inc(s_["w_exp"], 1)
                for g in range(NG):
                    act.wait_ge(s_["w_ready"], g + 1)
                    nc.scalar.activation(w_t_hi[:, g], w_t[:, g], ACT.Copy).then_inc(s_["w_hi_ready"], 1)
                for k in range(KT):
                    act.wait_ge(s_["mixed"], k + 1)
                    nc.scalar.activation(h_hi[:, k], mix_a[:, k % 2], ACT.Copy).then_inc(s_["o_hi"], 1)
                for u in range(st["o"].chunks):
                    split_next("o", 0, u)
                    residual_chunk("o", 0, u)

        def attention_vec(v, own, name, split_next, norm, residual_chunk):
            if name == "kv":
                norm(2, 2, 4, KV_SC)
                for j in range(st["kv"].chunks + 1):
                    i, u = divmod(j, UNROLL)
                    if j < st["kv"].chunks:
                        split_next("kv", i, u)
                    if 0 < j <= K_TILES // 2:
                        g = j - 1
                        norm_vec(v, 2 * g, g % 2, (48 + g, g), lambda t: in_residues(k_all[:, 2 * g + t], g))
                    elif j > K_TILES // 2:
                        g = j - 1 - K_TILES // 2
                        for t in range(2):
                            v.wait_ge(s_["v_tt"], 2 * g + t + 1)
                            nc.vector.tensor_copy(v_all[:, g, :, t * P:(t + 1) * P],
                                                  PS[4 + t][:, :].rearrange("p (b f) -> p b f", b=BLOCKS)).then_inc(s_["v_tok"], 1)
                    if j < K_TILES // 2:
                        squares_vec(v, 2 * j)
                    if j == st["kv"].chunks - 1:
                        norm(None, 3, 5, B0 + SC_M)
            elif name == "q":
                with v.Fori(0, NG) as i:
                    for u in range(UNROLL + 1):
                        if u < UNROLL:
                            split_next("q", i, u)
                        if u:
                            c = UNROLL * i + u - 1
                            norm_vec(v, K_TILES + 2 * c, (u - 1) % 2, (51 + i, 0), lambda t: q_all[:, 2 * UNROLL * i + 2 * (u - 1) + t])
                        if u < UNROLL:
                            c = UNROLL * i + u
                            squares_vec(v, K_TILES + 2 * c)
            else:
                v.wait_ge(s_["chunk_used"], Q_END)
                for g in range(NG):
                    with v.Fori(0, 2) as i:
                        base = BODY * (2 * g + i)
                        blocks = blocks_of(g)
                        for step in range(BODY + 2):
                            if step < BODY:
                                n, u, b, nk = blocks[step]
                                if n == 0:
                                    wait(v, "stat_kept", 2 * g + i)
                                v.wait_ge(s_["sc_ready"], base + n + 1)
                                wait(v, "pt_ps", base + n - 1)
                                mask = res_mask[:, :] if g == 2 else win_mask[:, :, :].rearrange("p b k -> p (b k)")[:, (2 - nk) * P:]
                                for side in range(2):
                                    last = nc.vector.tensor_tensor(
                                        probs[:, n % 2, side:REP:2, 0:nk * P],
                                        BANK[2 * (n % 2) + side][:, 0:2 * nk * P].rearrange("p (r k) -> p r k", r=2),
                                        mask.unsqueeze(1).broadcast_to([P, 2, nk * P]), ALU.add)
                                last.then_inc(s_["masked"], 1)
                                wait(v, "masked", base + n + 1)
                                nc.vector.tensor_reduce(out=stat[:, 0, u, b, :], in_=probs[:, n % 2, :, 0:nk * P],
                                                        axis=AX.X, op=ALU.max).then_inc(s_["max_ready"], 1)
                                v.wait_ge(s_["max_ready"], base + n + 1)
                                nc.vector.tensor_scalar(neg_max[:, u, b, :, 0], stat[:, 0, u, b, :], -1.0, None, ALU.mult).then_inc(s_["neg_ready"], 1)
                            if 0 < step <= BODY and blocks[step - 1][3] == 2:
                                n, u, b, nk = blocks[step - 1]
                                v.wait_ge(s_["pt_ps"], base + n + 1 + CREDIT["pt_ps"])
                                wait(v, "pv_ready", base + n - 1)
                                nc.vector.tensor_copy(probs_t[:, n % 2, 1].rearrange("p r q -> p (r q)"),
                                                      PS[5 - n % 2][:, :]).then_inc(s_["pt1_ready"], 1)
                            if step >= 2:
                                n, u, b, nk = blocks[step - 2]
                                wait(v, "pv_ready", base + n + 1)
                                for j in range(2):
                                    dst = by_residue(q_all[:, KT * g + 4 * i + 2 * u + j], g)
                                    src = PS[6 + n % 2][:, j * P:(j + 1) * P]
                                    if g == 0:
                                        dst = dst[:, 0, b * P:(b + 1) * P]
                                    elif g == 1:
                                        dst = dst[:, b]
                                    else:
                                        dst = dst[:, 4 * b:4 * b + 4]
                                        src = src.rearrange("p (r i) -> p r i", r=4)
                                    last = nc.vector.tensor_copy(dst, src)
                                last.then_inc(s_["o_kept"], 1)
                        v.wait_ge(s_["probs_ready"], base + BODY)
                        nc.vector.tensor_copy(max_all[:, g, :, :].rearrange("p b (i u) r -> p i u b r", u=2)[:, i], stat[:, 0])
                        nc.vector.tensor_copy(sum_all[:, g, :, :].rearrange("p b (i u) r -> p i u b r", u=2)[:, i], stat[:, 1]).then_inc(s_["stat_kept"], 1)
                for g in range(NG):
                    v.wait_ge(s_["stat_t"], 2 * g + 1)
                    own.mark(nc.vector.tensor_copy(by_residue(w_t[:, g], g), in_residues(PS[2 * g][0:QH, :], g)))
                own.wait()
                own.link(nc.vector.tensor_tensor(top[:, :], w_t[:, 0], w_t[:, 1], ALU.max))
                own.link(nc.vector.tensor_tensor(top[:, :], top[:, :], w_t[:, 2], ALU.max))
                for g in range(NG):
                    nc.vector.tensor_tensor(w_t[:, g], w_t[:, g], top[:, :], ALU.subtract).then_inc(s_["below_top"], 1)
                v.wait_ge(s_["sum_t_ready"], NG)
                for g in range(NG):
                    v.wait_ge(s_["w_exp"], g + 1)
                    own.mark(nc.vector.tensor_tensor(sum_t[:, g], sum_t[:, g], w_t[:, g], ALU.mult))
                own.wait()
                own.link(nc.vector.tensor_tensor(top[:, :], sum_t[:, 0], sum_t[:, 1], ALU.add))
                own.link(nc.vector.tensor_tensor(top[:, :], top[:, :], sum_t[:, 2], ALU.add))
                own.link(nc.vector.reciprocal(top[:, :], top[:, :]))
                for g in range(NG):
                    nc.vector.tensor_tensor(w_t[:, g], w_t[:, g], top[:, :], ALU.mult).then_inc(s_["w_ready"], 1)
                for g in range(NG):
                    v.wait_ge(s_["w_hi_ready"], g + 1)
                    v.wait_ge(s_["w_ready"], g + 1)
                    nc.vector.tensor_tensor(w_t_lo[:, g], w_t[:, g], w_t_hi[:, g].bitcast(F32), ALU.subtract).then_inc(s_["w_split"], 1)
                for k in range(KT + 1):
                    if k < KT:
                        if k >= 2:
                            v.wait_ge(s_["o_hi"], k - 1)
                            v.wait_ge(s_["o_ready"], k - 1)
                        v.wait_ge(s_["w_wide"], k + 1)
                        for g, mix in enumerate((mix_a, mix_b, mix_c)):
                            last = nc.vector.tensor_tensor(mix[:, k % 2], q_all[:, KT * g + k], PS[2 + NG * (k % 2) + g][:, :], ALU.mult)
                        last.then_inc(s_["weighed"], 1)
                    if k:
                        v.wait_ge(s_["o_hi"], k)
                        v.wait_ge(s_["mixed"], k)
                        nc.vector.tensor_tensor(h_lo[:, k - 1], mix_a[:, (k - 1) % 2], h_hi[:, k - 1].bitcast(F32), ALU.subtract).then_inc(s_["o_ready"], 1)
                for u in range(st["o"].chunks):
                    split_next("o", 0, u)
                    residual_chunk("o", 0, u)

        def attention_pe(pe, name, products, norm, before):
            if name == "kv":
                norm(2)
                wait(pe, *before)
                pe.wait_ge(s_["masks_ready"], 10)
                for j in range(st["kv"].chunks + 1):
                    i, u = divmod(j, UNROLL)
                    chunk = j < st["kv"].chunks
                    v_j = j - 1 - K_TILES // 2
                    if chunk and j >= 2:
                        if j - 2 < K_TILES // 2:
                            pe.wait_ge(s_["qk_done"], 2 * (j - 1))
                        else:
                            pe.wait_ge(s_["v_perm"], 2 * (j - 1) - K_TILES)
                    if j == st["kv"].chunks - 1:
                        for k in range(KT // 2):
                            products("kv", i, u, range(k, k + 1)).then_inc(s_["h_free"], 1)
                    elif chunk:
                        products("kv", i, u, range(0, KT // 2),
                                 ready=(lambda k: pe.wait_ge(s_["h_ready"], KT * 2 + k + 1)) if j == 0 else None)
                        if j == 0:
                            last = products("kv", i, u, range(KT // 2, KT), ready=lambda k: pe.wait_ge(s_["h_ready"], KT * 2 + k + 1))
                    if 0 < j <= K_TILES // 2:
                        sums_pe(pe, 2 * (j - 1), first=(j == 1))
                    elif v_j >= 0:
                        for t in range(2):
                            pe.wait_ge(s_["v_perm"], 2 * v_j + t + 1)
                            if v_j:
                                pe.wait_ge(s_["v_tok"], 2 * v_j - 1 + t)
                            for b in range(BLOCKS):
                                last_t = nc.tensor.transpose(PS[4 + t][:, b * P:(b + 1) * P], v_order[:, t, b * P:(b + 1) * P], ident[:, :])
                            last_t.then_inc(s_["v_tt"], 1)
                    if chunk:
                        if 0 < j < st["kv"].chunks - 1:
                            last = products("kv", i, u, range(KT // 2, KT))
                        elif j:
                            for k in range(KT // 2, KT):
                                last = products("kv", i, u, range(k, k + 1))
                                if k < KT - 1:
                                    last.then_inc(s_["h_free"], 1)
                        last.then_inc(s_["chunk_used"], 1)
                return None
            if name == "q":
                pe.wait_ge(s_["v_perm"], K_TILES)
                with pe.Fori(0, NG) as i:
                    for u in range(UNROLL):
                        c = UNROLL * i + u
                        pe.wait_ge(s_["qk_done"], K_TILES + 2 * (c - 1))
                        products("q", i, u, range(0, KT // 2),
                                 ready=(lambda k: pe.wait_ge(s_["h_ready"], KT * 3 + k + 1)) if u == 0 else None)
                        if u:
                            sums_pe(pe, K_TILES + 2 * (c - 1))
                        products("q", i, u, range(KT // 2, KT),
                                 ready=(lambda k: pe.wait_ge(s_["h_ready"], KT * 3 + k + 1)) if u == 0 else None).then_inc(s_["chunk_used"], 1)
                    sums_pe(pe, K_TILES + 2 * (UNROLL * i + UNROLL - 1))
                return None
            pe.wait_ge(s_["qk_done"], K_TILES + NG * QH // 2)
            pe.wait_ge(s_["v_tok"], K_TILES)
            for g in range(NG):
                if g == 1:
                    wait(pe, "pt0_ready", 2 * BODY)
                with pe.Fori(0, 2) as i:
                    base = BODY * (2 * g + i)
                    blocks = blocks_of(g)
                    for step in range(BODY + 2):
                        if step < BODY:
                            n, u, b, nk = blocks[step]
                            if b == 0:
                                wait(pe, "staged", KVH * g + 2 * i + u + 1)
                            wait(pe, "masked", base + n - 1)
                            for r in range(REP):
                                half_ = slice((r % 2) * HD, (r % 2) * HD + HD)
                                dst = BANK[2 * (n % 2) + r % 2][:, (r // 2) * nk * P:(r // 2 + 1) * nk * P]
                                last = nc.tensor.matmul(dst, q_u[half_, u, r // 2, b * P:(b + 1) * P],
                                                        k_u[half_, u, (b + 1 - nk) * P:(b + 1) * P], start=True, stop=True)
                            last.then_inc(s_["sc_ready"], 1)
                        if 0 < step <= BODY:
                            n, u, b, nk = blocks[step - 1]
                            pe.wait_ge(s_["probs_ready"], base + n + 1)
                            if g == 0:
                                wait(pe, "pt0_ready", base + n)
                                wait(pe, "pt1_ready", (BLOCKS - 1) * (2 * i + u) + max(b - 1, 0))
                            else:
                                wait(pe, "pt0_ready", base + n - 1)
                            for kb in range(nk):
                                bank = PS[4 + n % 2] if kb == 0 else PS[5 - n % 2]
                                for r in range(REP):
                                    last = nc.tensor.transpose(bank[:, r * P:(r + 1) * P], probs[:, n % 2, r, kb * P:(kb + 1) * P], ident[:, :])
                            last.then_inc(s_["pt_ps"], 1)
                        if step >= 2:
                            n, u, b, nk = blocks[step - 2]
                            wait(pe, "pt0_ready", base + n + 1)
                            if nk == 2:
                                wait(pe, "pt1_ready", (BLOCKS - 1) * (2 * i + u) + b)
                            wait(pe, "o_kept", base + n - 1)
                            for r in range(REP):
                                side, j = r % 2, r // 2
                                for kb in range(nk):
                                    last = nc.tensor.matmul(PS[6 + n % 2][side * HD:(side + 1) * HD, j * P:(j + 1) * P],
                                                            v_u[:, u, b + 1 - nk + kb], probs_t[:, n % 2, kb, r],
                                                            start=(kb == 0), stop=(kb == nk - 1))
                            last.then_inc(s_["pv_ready"], 1)
            wait(pe, "stat_kept", 2 * NG)
            wait(pe, "o_kept", BODY * 2 * NG)
            for g in range(NG):
                for kind, src in enumerate((max_all, sum_all)):
                    for b in range(BLOCKS):
                        last = nc.tensor.transpose(PS[2 * g + kind][0:QH, b * P:(b + 1) * P],
                                                   src[:, g, b].rearrange("p h r -> p (h r)"), ident[:, :])
                    last.then_inc(s_["stat_t"], 1)
            for k in range(KT + 2):
                if k < KT:
                    if k >= 2:
                        pe.wait_ge(s_["weighed"], k - 1)
                    for g in range(NG):
                        if k == 0:
                            pe.wait_ge(s_["w_split"], g + 1)
                        wide = PS[2 + NG * (k % 2) + g][:, :]
                        nc.tensor.matmul(wide, head_row[:, k], w_t_hi[:, g], start=True, stop=False)
                        last = nc.tensor.matmul(wide, head_row[:, k], w_t_lo[:, g], start=False, stop=True)
                    last.then_inc(s_["w_wide"], 1)
                if k >= 2:
                    last = products("o", 0, 0, range(k - 2, k - 1), ready=lambda kk: pe.wait_ge(s_["o_ready"], kk + 1))
            last.then_inc(s_["chunk_used"], 1)
            pe.wait_ge(s_["weighed"], KT)
            for u in range(1, st["o"].chunks):
                if u >= 2:
                    wait(pe, "x_new", X0["o"] + 2 * (u - 1))
                products("o", 0, u).then_inc(s_["chunk_used"], 1)
            return ("x_new", X0["o"] + KT)

        @block.sync
        def _(sp):
            vec_rows = [(0, 48, 0, ins["a_ada_b"][0]), (48, 96, 0, ins["b_ada_b"][0]), (96, 112, 0, ins["kv_ada_b"]),
                        (112, 120, 0, ins["c"][0]), (0, 32, 2, ins["a_conv_b"][0]), (32, 48, 2, ins["a_norm_w"][0])]
            for a, b, j, src in vec_rows:
                sp.dma_start(pre[a:b, j], src.rearrange("(n p) -> n p", p=P)).then_inc(s_["vec_in"], 16)
            sp.dma_start(pre[:, 1], ins["a_conv_w"][0].rearrange("t (n p) -> (t n) p", p=P)).then_inc(s_["vec_in"], 16)
            for r, src in ((48, ins["k_norm"]), (51, ins["b_q_norm"][0])):
                for side in range(2):
                    sp.dma_start(pre[r:r + NG, 2, side * HD:(side + 1) * HD], src).then_inc(s_["vec_in"], 16)

            def load(s, src, i, per):
                slot = s % SLOTS
                if isinstance(i, int):
                    if s + i * per >= SLOTS:
                        kind, n = owner[s + i * per - SLOTS]
                        sp.wait_ge(s_["chunk_used" if kind == "m" else "ada_used"], n + 1)
                else:
                    kind, n = owner[s - SLOTS]
                    sp.wait_ge(s_["chunk_used" if kind == "m" else "ada_used"], n + 1 + i * UNROLL)
                dst = raw[:, slot].rearrange("p (k c) -> p k c", c=CW) if len(src.shape) == 3 else raw[:, slot]
                sp.dma_start(dst, src).then_inc(raw_in[slot], 16)

            for k in range(A0_LOADS):
                if k == 2:
                    for b in range(NCH):
                        sp.dma_start(x_in[:, b], ins["x"][0, b * P:(b + 1) * P, :]).then_inc(x_loaded[b], 16)
                load(k, ada_a[:, k, 0], 0, 0)

            def regular(name):
                s = st[name]
                per = UNROLL * s.lpc
                return s.chunks % UNROLL == 0 and all(
                    owner[s.l0 + u - SLOTS + i * per] == (owner[s.l0 + u - SLOTS][0], owner[s.l0 + u - SLOTS][1] + i * UNROLL)
                    for u in range(per) for i in range(s.chunks // UNROLL))

            for name in STAGES:
                s = st[name]

                def body(i, units):
                    for u in range(units):
                        load(s.l0 + s.lpc * u, main_src(name, i, u), i, UNROLL * s.lpc)
                        if s.lpc == 2:
                            w, g, _ = ADA[name]
                            load(s.l0 + 2 * u + 1, w[:, UNROLL * i + u, g], i, UNROLL * s.lpc)

                if regular(name):
                    bodies(sp, name, body)
                else:
                    for i in range(0, s.chunks, UNROLL):
                        body(i // UNROLL, min(UNROLL, s.chunks - i))
            for b in range(NCH):
                sp.wait_ge(s_["out_sb"], 2 * (b + 1))
                sp.dma_start(out[0, b * P:(b + 1) * P, :], fin[:, b]).then_inc(s_["out_sem"], 16)
            sp.wait_ge(s_["out_sem"], 16 * NCH)

        @block.gpsimd
        def _(pool):
            pool.dma_start(dt_bias[:, :], ins["a_dt_bias"].rearrange("a h -> h a"), allow_slow_non_contiguous=True).then_inc(s_["pool_in"], 16)
            pool.dma_start(a_exp[:, :], ins["a_A_log"][0].partition_broadcast(P)).then_inc(s_["pool_in"], 16)
            pool.dma_start(d_row[:, :], ins["a_D"][0].rearrange("(t two) -> two t", two=2), allow_slow_non_contiguous=True).then_inc(s_["pool_in"], 16)
            pool.dma_start(dt_w[:, :, :], w_in[:, 3 * DI:3 * DI + HEADS].rearrange("(k p) c -> p k c", p=P)).then_inc(s_["pool_in"], 16)
            pool.memset(acc[:, :], 0.0).then_inc(s_["ada_zero"], 1)
            own = s_["consts"]
            pool.memset(ident[:, :], 0.0).then_inc(own, 1)
            pool.memset(ones[:, :], 1.0).then_inc(own, 1)
            pool.memset(tri[:, :], 1.0).then_inc(own, 1)
            pool.memset(negm[:, :], 0.0).then_inc(own, 1)
            pool.memset(half[:, :], 1.0).then_inc(own, 1)
            pool.memset(ssum[:, :], 0.0).then_inc(own, 1)
            pool.wait_ge(own, 6)
            pool.affine_select(out=ident[:, :], in_=ident[:, :], compare_op=ALU.not_equal, fill=1.0, base=0,
                               pattern=[[-1, P]], channel_multiplier=1).then_inc(own, 1)
            pool.affine_select(out=tri[:, :], in_=tri[:, :], compare_op=ALU.is_ge, fill=0.0, base=0,
                               pattern=[[1, P]], channel_multiplier=-1).then_inc(own, 1)
            pool.affine_select(out=negm[:, :], in_=negm[:, :], compare_op=ALU.is_ge, fill=NEG, base=0,
                               pattern=[[1, P]], channel_multiplier=-1).then_inc(own, 1)
            pool.affine_select(out=half[:, :], in_=half[:, :], compare_op=ALU.is_ge, fill=0.0, base=0,
                               pattern=[[1, P]], channel_multiplier=-HD).then_inc(own, 1)
            pool.wait_ge(own, 10)
            pool.affine_select(out=half[:, :], in_=half[:, :], compare_op=ALU.is_ge, fill=0.0, base=HD - 1,
                               pattern=[[-1, P]], channel_multiplier=HD).then_inc(own, 1)

            def add_square(n, k, slot, first=False):
                if first and n:
                    pool.wait_ge(s_["ms_ready"], n)
                pool.wait_ge(s_["sq_ready"], KT * n + k + 1)
                if first:
                    pool.tensor_copy(ssum[:, :], sq[:, slot]).then_inc(s_["ss_done"], 1)
                else:
                    pool.wait_ge(s_["ss_done"], KT * n + k)
                    pool.tensor_tensor(ssum[:, :], ssum[:, :], sq[:, slot], ALU.add).then_inc(s_["ss_done"], 1)

            def norm_of(n):
                for k in range(KT):
                    add_square(n, k, k % 2, first=(k == 0))

            for at_, name in enumerate(n for n, count in CREDIT.items() for _ in range(count)):
                pool.memset(credit[:, at_:at_ + 1], 0.0).then_inc(s_[name], 1)
            norm_of(0)
            group_no = 1
            for name in STAGES:
                if st[name].lpc == 2:
                    pool.wait_ge(s_["ada_sum"], group_no)
                    pool.memset(acc[:, :], 0.0).then_inc(s_["ada_zero"], 1)
                    group_no += 1
                if name == "z":
                    scan_pool(pool)
                if name == "kv":
                    attention_masks(pool)
                if name == "o":
                    attention_pool(pool)
                if name in NORM_OF:
                    norm_of(NORM_OF[name])

        @block.scalar
        def _(act):
            def split_hi(s, i, u):
                slot = (s.l0 + s.lpc * u) % SLOTS
                act.wait_ge(raw_in[slot], 16 * ((s.l0 + s.lpc * u) // SLOTS + i * s.lpc + 1))
                m = s.m0 + u + UNROLL * i
                if s.m0 + u >= 2:
                    wait(act, "chunk_used", m - 1)
                nc.scalar.activation(w_hi[:, (s.m0 + u) % 2], raw[:, slot], ACT.Copy).then_inc(s_["hi_ready"], 1)

            def split_next(name, i, u):
                last = name == LAST and u == UNROLL - 1
                s = st[name]
                if not last:
                    split_hi(s, i, u + 1)
                elif isinstance(i, int) and UNROLL * i + u + 1 < s.chunks:
                    split_hi(s, i, u + 1)

            def square(n, k, slot, src):
                if n or k >= 2:
                    wait(act, "ss_done", KT * n + k - 1)
                nc.scalar.activation(sq[:, slot], src, ACT.Square).then_inc(s_["sq_ready"], 1)

            def norm(n, v, free, table, shift):
                if n is not None:
                    wait(act, "ms_ready", n + 1)
                    nc.scalar.activation(root[:, :], NB[:, :], ACT.Ln, bias=EPS, scale=1.0 / D).then_inc(s_["root_ready"], 1)
                    wait(act, "root_ready", n + 1)
                    nc.scalar.activation(rstd[:, :], root[:, :], ACT.Exp, scale=-0.5).then_inc(s_["rstd_ready"], 1)
                if free:
                    wait(act, "chunk_used", free)
                wait(act, "ada_tab", table)
                for k in range(KT):
                    if free is None:
                        wait(act, "h_free", k + 1) if k < KT - 1 else wait(act, "chunk_used", KV_END)
                    wait(act, "mod_ready", KT * v + k + 1)
                    nc.scalar.activation(h_hi[:, k], mod[:, k % 2], ACT.Identity, bias=ada[:, shift + k]).then_inc(s_["h_hi_ready"], 1)

            wait(act, "vec_ok", 3)
            nc.scalar.activation(csil[:, :, 0], vecs[:, 112:120, 0], ACT.Silu).then_inc(s_["cs_ok"], 1)
            for k in range(KT):
                wait(act, "x_new", k + 1)
                square(0, k, k % 2, xT[:, k])
            split_hi(st["x"], 0, 0)
            norm(0, 0, 0, 1, SH_M)

            def conv_chunk(name, i, u):
                s = st[name]
                m = s.m0 + UNROLL * i + u
                done = CONV0[name] + 2 * (UNROLL * i + u)
                wait(act, "chunk_used", m + 1)
                for t in range(2):
                    tile, dst = conv_tile(name, i, u, t)
                    nc.scalar.activation(conv[:, dst], BANK[2 * (u % 2) + t][:, :], ACT.Identity,
                                         bias=vec2[:, tile], scale=taps[:, TAPS - 1, tile]).then_inc(s_["tap0"], 1)
                for t in range(2):
                    _, dst = conv_tile(name, i, u, t)
                    wait(act, "conv_sum", done + t + 1)
                    nc.scalar.activation(conv[:, dst], conv[:, dst], ACT.Silu).then_inc(s_["conv_ready"], 1)

            def hidden_chunk(name, i, u):
                s = st[name]
                done = HID0[name] + 2 * (UNROLL * i + u)
                wait(act, "chunk_used", s.m0 + UNROLL * i + u + 1)
                for t in range(2):
                    wait(act, "hid_ready", done + t - 1)
                    nc.scalar.activation(relu[:, t], BANK[2 * (u % 2) + t][:, :], ACT.Relu).then_inc(s_["relu_ready"], 1)
                for t in range(2):
                    hi = 4 * UNROLL * i + 4 * u + 2 + t
                    wait(act, "relu_ready", done + t + 1)
                    nc.scalar.activation(big[:, hi], relu[:, t], ACT.Square).then_inc(s_["hid_hi"], 1)

            def residual_chunk(name, i, u):
                if name in NORM_OF and (u % st[name].kg == st[name].kg - 1):
                    per = UNROLL // st[name].kg
                    for t in range(2):
                        k = 2 * (per * i + u // st[name].kg) + t
                        wait(act, "x_new", X0[name] + k + 1)
                        square(NORM_OF[name], k, t, xT[:, k])

            for name in STAGES:
                if name == "z":
                    scan_act(act, split_next)
                    continue
                if name in ("kv", "q", "o"):
                    attention_act(act, name, split_next, norm, residual_chunk)
                    continue
                if name in ("m1a", "n1a"):
                    b = name == "n1a"
                    norm(3 if b else 1, 4 if b else 1, st["o" if b else "z"].m0 + st["o" if b else "z"].chunks, 7 if b else 3,
                         (B0 if b else 0) + SH_F)

                def body(i, units):
                    for u in range(units):
                        split_next(name, i, u)
                        if name == "bc":
                            step_sizes_act(act, UNROLL * i + u)
                        if name in ("x", "bc"):
                            conv_chunk(name, i, u)
                        elif name in HID0:
                            hidden_chunk(name, i, u)
                        else:
                            residual_chunk(name, i, u)

                if name == "bc" or name == LAST:
                    for i in range(st[name].chunks // UNROLL):
                        body(i, UNROLL)
                else:
                    bodies(act, name, body)
        @block.vector
        def _(v):
            own = Chain(v, s_["dve_own"])

            def split_lo(s, i, u):
                slot = (s.l0 + s.lpc * u) % SLOTS
                v.wait_ge(s_["hi_ready"], s.m0 + u + UNROLL * i + 1)
                nc.vector.tensor_tensor(w_lo[:, slot], raw[:, slot], w_hi[:, (s.m0 + u) % 2].bitcast(F32),
                                        ALU.subtract).then_inc(s_["lo_ready"], 1)

            def split_next(name, i, u):
                s = st[name]
                if not (name == LAST and u == UNROLL - 1) or (isinstance(i, int) and UNROLL * i + u + 1 < s.chunks):
                    split_lo(s, i, u + 1)

            def ada_step(load, k, a, per, i):
                slot = load % SLOTS
                v.wait_ge(raw_in[slot], 16 * (load // SLOTS + i * per // SLOTS + 1) if isinstance(i, int)
                          else 16 * (load // SLOTS + 1) + i * (16 * per // SLOTS))
                if not isinstance(i, int) or i or a:
                    v.wait_ge(s_["ada_used"], a + i * UNROLL)
                nc.vector.scalar_tensor_tensor(out=acc[:, :], in0=raw[:, slot], scalar=csil[:, k], in1=acc[:, :],
                                               op0=ALU.mult, op1=ALU.add).then_inc(s_["ada_used"], 1)

            def ada_begin(n):
                v.wait_ge(s_["ada_zero"], n + 1)

            def ada_end(n, col):
                v.wait_ge(s_["ada_sum"], n + 1)
                nc.vector.tensor_tensor(ada[:, col:col + 16, 0], MB[:, 0:16], vecs[:, col:col + 16, 0], ALU.add).then_inc(s_["ada_tab"], 1)

            def norm(n, v_, table, scale):
                if n is not None:
                    v.wait_ge(s_["rstd_ready"], n + 1)
                v.wait_ge(s_["ada_tab"], table)

                def scaled(k):
                    if k >= 2:
                        v.wait_ge(s_["h_ready"], KT * v_ + k - 1)
                    nc.vector.scalar_tensor_tensor(out=mod[:, k % 2], in0=xT[:, k], scalar=ada[:, scale + k], in1=rstd[:, :],
                                                   op0=ALU.mult, op1=ALU.mult).then_inc(s_["mod_ready"], 1)

                scaled(0)
                for k in range(KT):
                    if k + 1 < KT:
                        scaled(k + 1)
                    v.wait_ge(s_["h_hi_ready"], KT * v_ + k + 1)
                    v.wait_ge(s_["mod_ready"], KT * v_ + k + 1)
                    nc.vector.scalar_tensor_tensor(out=h_lo[:, k], in0=mod[:, k % 2], scalar=ada[:, scale - KT + k],
                                                   in1=h_hi[:, k].bitcast(F32), op0=ALU.add, op1=ALU.subtract).then_inc(s_["h_ready"], 1)

            v.wait_ge(s_["vec_t"], 3)
            vt = vecs[:, :, 0]
            nc.vector.tensor_copy(vt, MB[:, 0:120]).then_inc(s_["vec_ok"], 1)
            nc.vector.tensor_copy(taps[:, :, :, 0], MB[:, P:2 * P].rearrange("p (t n) -> p t n", t=TAPS)).then_inc(s_["vec_ok"], 1)
            nc.vector.tensor_copy(vec2[:, :, 0], MB[:, 2 * P:2 * P + 54]).then_inc(s_["vec_ok"], 1)
            v.wait_ge(s_["vec_ok"], 3)
            for col in (SC_M, SC_F, B0 + SC_M, B0 + SC_F, KV_SC):
                own.link(nc.vector.tensor_scalar(vecs[:, col:col + KT, 0], vecs[:, col:col + KT, 0], 1.0, None, ALU.add))
            ada_begin(0)
            v.wait_ge(s_["cs_ok"], 1)
            for k in range(A0_LOADS):
                if k >= 2:
                    for t in ((2 * (k - 2), 2 * (k - 2) + 1) if k < 6 else ()):
                        v.wait_ge(s_["xt_t"], t + 1)
                        nc.vector.tensor_copy(xT[:, t], BANK[t % 4][:, :]).then_inc(s_["x_new"], 1)
                ada_step(k, k, k, 0, 0)
            split_lo(st["x"], 0, 0)
            ada_end(0, 0)
            norm(0, 0, 1, SC_M)

            def conv_chunk(name, i, u):
                banks = [BANK[2 * (u % 2) + t] for t in range(2)]
                tiles = [conv_tile(name, i, u, t) for t in range(2)]
                done = CONV0[name] + 2 * (UNROLL * i + u)
                for shift in range(1, TAPS):
                    for t in range(2):
                        tile, dst = tiles[t]
                        if shift == 1:
                            v.wait_ge(s_["tap0"], done + t + 1)
                        else:
                            own.wait_back(1 if shift < TAPS - 1 else 1 - t)
                        ins_ = nc.vector.scalar_tensor_tensor(
                            out=conv[:, dst, shift:S], in0=banks[t][:, 0:S - shift], scalar=taps[:, TAPS - 1 - shift, tile],
                            in1=conv[:, dst, shift:S], op0=ALU.mult, op1=ALU.add)
                        if shift < TAPS - 1:
                            own.mark(ins_)
                        else:
                            ins_.then_inc(s_["conv_sum"], 1)

            def hidden_chunk(name, i, u):
                done = HID0[name] + 2 * (UNROLL * i + u)
                for t in range(2):
                    wait(v, "relu_ready", done + t + 1)
                    own.mark(nc.vector.tensor_tensor(mod[:, t], relu[:, t], relu[:, t], ALU.mult))
                for t in range(2):
                    lo = 4 * UNROLL * i + 4 * u + t
                    v.wait_ge(s_["hid_hi"], done + t + 1)
                    own.wait_back(1 - t)
                    nc.vector.tensor_tensor(big[:, lo], mod[:, t], big[:, lo + 2].bitcast(F32), ALU.subtract).then_inc(s_["hid_ready"], 1)

            def residual_chunk(name, i, u):
                kg = st[name].kg
                if u % kg == kg - 1:
                    gate = {"out": G_M, "m": G_F, "o": B0 + G_M, "n": B0 + G_F}[name if name in ("out", "o") else name[0]]
                    pair = (UNROLL // kg) * i + u // kg
                    v.wait_ge(s_["chunk_used"], st[name].m0 + UNROLL * i + u + 1)
                    for t in range(2):
                        k = 2 * pair + t
                        bank = BANK[2 * ((u // kg) % 2) + t]
                        nc.vector.scalar_tensor_tensor(out=xT[:, k], in0=bank[:, :], scalar=ada[:, gate + k], in1=xT[:, k],
                                                       op0=ALU.mult, op1=ALU.add).then_inc(s_["x_new"], 1)

            group_no = 1
            for name in STAGES:
                s = st[name]
                if name == "z":
                    scan_vec(v, own, split_next)
                    continue
                if name in ("kv", "q", "o"):
                    attention_vec(v, own, name, split_next, norm, residual_chunk)
                    continue
                if name in ("m1a", "n1a"):
                    b = name == "n1a"
                    norm(3 if b else 1, 4 if b else 1, 7 if b else 3, (B0 if b else 0) + SC_F)
                if s.lpc == 2:
                    ada_begin(group_no)

                def body(i, units):
                    for u in range(units):
                        if s.lpc == 2:
                            ada_step(s.l0 + 2 * u + 1, UNROLL * i + u, s.a0 + u, 2 * UNROLL, i)
                        split_next(name, i, u)
                        if name == "bc":
                            step_sizes_vec(v, own, UNROLL * i + u)
                        if name in ("x", "bc"):
                            conv_chunk(name, i, u)
                        elif name in HID0:
                            hidden_chunk(name, i, u)
                        else:
                            residual_chunk(name, i, u)

                links = {"x": 4, "bc": 4}.get(name, 2 if name in HID0 else 0) * UNROLL
                n = s.chunks // UNROLL
                if name != LAST and name != "bc":
                    with v.Fori(0, n) as i:
                        own.enter(i, links)
                        body(i, UNROLL)
                    own.leave(n)
                else:
                    for i in range(n):
                        body(i, UNROLL)
                if s.lpc == 2:
                    ada_end(group_no, ADA[name][2])
                    group_no += 1
            for b in range(NCH):
                for q in range(2):
                    v.wait_ge(s_["out_t"], 2 * b + q + 1)
                    nc.vector.tensor_copy(fin[:, b, q * S:(q + 1) * S], BANK[(2 * b + q) % 4][:, :]).then_inc(s_["out_sb"], 1)

        @block.tensor
        def _(pe):
            def products(name, i, u, ks=range(KT), group=0, groups=1, ready=None):
                s = st[name]
                slot, hs = (s.l0 + s.lpc * u) % SLOTS, (s.m0 + u) % 2
                pair = (u // s.kg) % 2
                if ks[0] == 0:
                    pe.wait_ge(s_["lo_ready"], s.m0 + UNROLL * i + u + 1)
                for k in ks:
                    if ready:
                        ready(k)
                    if name in ("out", "m2a", "m2b", "n2a", "n2b"):
                        lo, hi = tile_at(KT * group + k)
                        xh, xl = big[:, hi], big[:, lo]
                    else:
                        xh, xl = h_hi[:, k], h_lo[:, k]
                    for t in range(2):
                        at_ = slice(k * CW + t * P, k * CW + (t + 1) * P)
                        dst = BANK[2 * pair + t][:, :]
                        first, final = (k == 0 and group == 0), (k == KT - 1 and group == groups - 1)
                        nc.tensor.matmul(dst, w_hi[:, hs, at_], xh, start=first, stop=False)
                        nc.tensor.matmul(dst, w_hi[:, hs, at_], xl, start=False, stop=False)
                        last = nc.tensor.matmul(dst, w_lo[:, slot, at_], xh, start=False, stop=final)
                return last

            def ada_reduce(n, used):
                pe.wait_ge(s_["ada_used"], used)
                if n:
                    pe.wait_ge(s_["ada_tab"], n)
                for j in range(2 * KT):
                    last = nc.tensor.matmul(MB[:, j:j + 1], acc[:, j * P:(j + 1) * P], ones[:, 0:1], start=True, stop=True)
                last.then_inc(s_["ada_sum"], 1)

            def norm(n):
                pe.wait_ge(s_["ss_done"], KT * (n + 1))
                nc.tensor.matmul(NB[:, :], ones[:, :], ssum[:, :], start=True, stop=True).then_inc(s_["ms_ready"], 1)

            pe.wait_ge(s_["consts"], 11)
            pe.wait_ge(s_["vec_in"], ROWS_IN)
            nc.tensor.transpose(MB[:, 0:120], pre[0:120, 0], ident[0:120, 0:120]).then_inc(s_["vec_t"], 1)
            nc.tensor.transpose(MB[:, P:2 * P], pre[:, 1], ident[:, :]).then_inc(s_["vec_t"], 1)
            nc.tensor.transpose(MB[:, 2 * P:2 * P + 54], pre[0:54, 2], ident[0:54, 0:54]).then_inc(s_["vec_t"], 1)
            for b in range(NCH):
                pe.wait_ge(x_loaded[b], 16)
            for k in range(KT):
                if k >= 4:
                    pe.wait_ge(s_["x_new"], k - 3)
                for b in range(NCH):
                    last = nc.tensor.transpose(BANK[k % 4][:, b * P:(b + 1) * P], x_in[:, b, k * P:(k + 1) * P], ident[:, :])
                last.then_inc(s_["xt_t"], 1)
            norm(0)
            ada_reduce(0, KT)

            def freed(name):
                if name in CONV0:
                    return "conv_sum", CONV0[name]
                if name in HID0:
                    return "relu_ready", HID0[name]
                return "x_new", X0[name]

            modulated = {"x": 0, "m1a": 1, "n1a": 4}
            before = ("x_new", KT)
            group_no = 1
            for name in STAGES:
                s = st[name]
                if name == "z":
                    last_group_sum = scan_pe(pe, products)
                    before = None
                    continue
                if name in ("kv", "q", "o"):
                    before = attention_pe(pe, name, products, norm, before)
                    continue
                if name in ("m1a", "n1a"):
                    norm(3 if name == "n1a" else 1)
                if before:
                    wait(pe, *before)
                sig, base = freed(name)

                def body(i, units):
                    for u in range(units):
                        pair = (UNROLL // s.kg) * i + u // s.kg
                        if name == "bc":
                            step_sizes_pe(pe, UNROLL * i + u)
                        if name == "out" and i == 0:
                            if u % 2 == 0:
                                wait(pe, "z_ready", 2 * GROUPS - 2 + u)
                                wait(pe, "groot_ready", GROUPS - 1 + u // 2)
                            if u == 0:
                                products(name, 0, 0, range(0, KT // 2), groups=s.kg, ready=lambda k: wait(pe, "y_out", k + 1))
                                last_group_sum()
                                products(name, 0, 0, range(KT // 2, KT), groups=s.kg,
                                         ready=lambda k: wait(pe, "y_out", k + 1)).then_inc(s_["chunk_used"], 1)
                                continue
                        if u % s.kg == 0 and not (name == "out" and pair == 0):
                            wait(pe, sig, base + 2 * (pair - 1))
                        if name in modulated and u == 0:
                            def ready(k):
                                pe.wait_ge(s_["h_ready"], KT * modulated[name] + k + 1)
                        elif name == "out" and u < 2:
                            def ready(k):
                                wait(pe, "y_out", KT * u + k + 1)
                        elif name[1:2] == "2" and u < 2:
                            def ready(k):
                                wait(pe, "hid_ready", HID0[name[0] + "1" + name[2]] + KT * u + k + 1)
                        else:
                            ready = None
                        products(name, i, u, group=u % s.kg, groups=s.kg, ready=ready).then_inc(s_["chunk_used"], 1)

                if name in ("bc", "out"):
                    for i in range(s.chunks // UNROLL):
                        body(i, UNROLL)
                else:
                    bodies(pe, name, body)
                if s.lpc == 2:
                    ada_reduce(group_no, s.a0 + s.chunks)
                    group_no += 1
                before = (sig, base + 2 * (s.chunks // s.kg))
            wait(pe, *before)
            for b in range(NCH):
                for q in range(2):
                    n = 2 * b + q
                    if n >= 4:
                        pe.wait_ge(s_["out_sb"], n - 3)
                    for j in range(4):
                        last = nc.tensor.transpose(BANK[n % 4][:, j * P:(j + 1) * P], xT[:, 4 * q + j, b * P:(b + 1) * P], ident[:, :])
                    last.then_inc(s_["out_t"], 1)


_INS = ["x", "c", "a_ada_w", "a_ada_b", "a_w_in", "a_conv_w", "a_conv_b", "a_dt_bias", "a_A_log", "a_D",
        "a_norm_w", "a_w_out", "a_mlp_w1", "a_mlp_w2", "kv_ada_w", "kv_ada_b", "kv_w", "k_norm",
        "b_ada_w", "b_ada_b", "b_w_q", "b_q_norm", "b_w_o", "b_mlp_w1", "b_mlp_w2"]


def kernel(**inputs):
    import numpy as np
    import concourse.bacc as bacc
    from concourse.bass_utils import run_bass_kernel_spmd

    nc = bacc.Bacc("TRN2", target_bir_lowering=False, num_devices=1)
    arrays, aps = {}, {}
    for name in _INS:
        a = np.ascontiguousarray(inputs[name])
        arrays["in_" + name] = a
        aps[name] = nc.dram_tensor("in_" + name, a.shape, mybir.dt.from_np(a.dtype), kind="ExternalInput").ap()
    out = nc.dram_tensor("out_x", (1, S, D), F32, kind="ExternalOutput").ap()
    trunk(nc, aps, out)
    r = run_bass_kernel_spmd(nc, [arrays], core_ids=[0])
    return r.results[0]["out_x"]
```
